# Optimizing a Trainium2 kernel written in Bass

```python
import math
import jax, jax.numpy as jnp
from jax import lax
import numpy as np

D_MODEL = 1024
BATCH = 1
SEQ = 512
DEPTH = 1

CHUNK = 64
SSD_DIM = D_MODEL
SSD_HEAD_DIM = 64
SSD_HEADS = SSD_DIM // SSD_HEAD_DIM
SSD_NGROUPS = 2
SSD_STATE = 128
SSD_CONV = 4
POOL_DIM = D_MODEL
POOL_WINDOWS = (2, 4, 8, 16)
POOL_GROUPS = len(POOL_WINDOWS)
POOL_GROUP_DIM = POOL_DIM // POOL_GROUPS
MIX_DIM = SSD_DIM + POOL_DIM
CONV_DIM = SSD_DIM + 2 * SSD_NGROUPS * SSD_STATE
IN_DIM = SSD_DIM + CONV_DIM + SSD_HEADS + POOL_DIM
D_FF = 2816
NORM_EPS = 1e-6

kernel_name = "hybrid_ssd_pool_macaron_block"

def rms_norm(x, g):
    xf = x.astype(jnp.float32)
    y = xf * lax.rsqrt(jnp.mean(xf * xf, axis=-1, keepdims=True) + NORM_EPS)
    return (y * g.astype(jnp.float32)).astype(x.dtype)

def swiglu(h, w_gate, w_up, w_down):
    return (jax.nn.silu(h @ w_gate) * (h @ w_up)) @ w_down

def causal_depthwise_conv(u, w, b):
    c = u.shape[-1]
    y = lax.conv_general_dilated(
        u, w.astype(u.dtype)[:, None, :], window_strides=(1,),
        padding=[(SSD_CONV - 1, 0)], dimension_numbers=('NWC', 'WIO', 'NWC'),
        feature_group_count=c)
    return y + b.astype(u.dtype)

def ssd_chunked_scan(xh, dt, A, Bh, Ch):
    b, s, h, p = xh.shape
    n = Bh.shape[-1]
    c = s // CHUNK
    X = (xh * dt[..., None]).reshape(b, c, CHUNK, h, p)
    Bc = Bh.reshape(b, c, CHUNK, h, n)
    Cc = Ch.reshape(b, c, CHUNK, h, n)
    A_cs = jnp.cumsum((dt * A).reshape(b, c, CHUNK, h).transpose(0, 3, 1, 2), axis=-1)
    causal = jnp.tril(jnp.ones((CHUNK, CHUNK), dtype=bool))
    L = jnp.exp(jnp.where(causal, A_cs[..., :, None] - A_cs[..., None, :], -jnp.inf))
    y_diag = jnp.einsum('bclhn,bcshn,bhcls,bcshp->bclhp', Cc, Bc, L, X)
    decay_states = jnp.exp(A_cs[..., -1:] - A_cs)
    states = jnp.einsum('bclhn,bhcl,bclhp->bchpn', Bc, decay_states, X)
    chunk_decay = jnp.exp(A_cs[..., -1])

    def step(carry, inp):
        st, dec = inp
        return dec[..., None, None] * carry + st, carry

    _, prev = lax.scan(step, jnp.zeros((b, h, p, n), jnp.float32),
                       (states.transpose(1, 0, 2, 3, 4), chunk_decay.transpose(2, 0, 1)))
    prev = prev.transpose(1, 0, 2, 3, 4)
    y_off = jnp.einsum('bclhn,bchpn,bhcl->bclhp', Cc, prev, jnp.exp(A_cs))
    return (y_diag + y_off).reshape(b, s, h, p)

def ssd_group(z, xbc, dt_raw, conv_w, conv_b, dt_bias, a_log, d_skip, ssd_norm):
    b, s, _ = z.shape
    xbc = jax.nn.silu(causal_depthwise_conv(xbc, conv_w, conv_b)).astype(jnp.float32)
    gn = SSD_NGROUPS * SSD_STATE
    xs = xbc[..., :SSD_DIM].reshape(b, s, SSD_HEADS, SSD_HEAD_DIM)
    rep = SSD_HEADS // SSD_NGROUPS
    Bh = jnp.repeat(xbc[..., SSD_DIM:SSD_DIM + gn].reshape(b, s, SSD_NGROUPS, SSD_STATE), rep, axis=2)
    Ch = jnp.repeat(xbc[..., SSD_DIM + gn:].reshape(b, s, SSD_NGROUPS, SSD_STATE), rep, axis=2)
    dt = jax.nn.softplus(dt_raw.astype(jnp.float32) + dt_bias.astype(jnp.float32))
    A = -jnp.exp(a_log.astype(jnp.float32))
    y = ssd_chunked_scan(xs, dt, A, Bh, Ch) + d_skip.astype(jnp.float32)[:, None] * xs
    yg = (y.reshape(b, s, SSD_DIM) * jax.nn.silu(z.astype(jnp.float32))).reshape(b, s, SSD_NGROUPS, -1)
    yg = yg * lax.rsqrt(jnp.mean(yg * yg, axis=-1, keepdims=True) + NORM_EPS)
    return (yg.reshape(b, s, SSD_DIM) * ssd_norm.astype(jnp.float32)).astype(z.dtype)

def multiscale_pool_group(u, pool_w, pool_scale):
    b, s, _ = u.shape
    uf = u.astype(jnp.float32).reshape(b, s, POOL_GROUPS, POOL_GROUP_DIM)
    csp = jnp.pad(jnp.cumsum(uf, axis=1), ((0, 0), (1, 0), (0, 0), (0, 0)))
    t = jnp.arange(s)
    outs = []
    for gi, win in enumerate(POOL_WINDOWS):
        cg = csp[:, :, gi]
        lo = jnp.pad(cg[:, :s + 1 - win], ((0, 0), (win - 1, 0), (0, 0)))
        cnt = jnp.minimum(t + 1, win).astype(jnp.float32)[None, :, None]
        outs.append((cg[:, 1:] - lo) / cnt - uf[:, :, gi])
    pooled = jnp.stack(outs, axis=2)
    y = jnp.einsum('bsgc,gcd->bsgd', pooled, pool_w.astype(jnp.float32)).reshape(b, s, POOL_DIM)
    return (y * pool_scale.astype(jnp.float32)).astype(u.dtype)

def setup_inputs(seed: int = 0) -> dict:
    key = jax.random.key(seed)
    ks = jax.random.split(key, 24)
    f32 = jnp.float32

    def nrm(k, shape, scale):
        return jax.random.normal(k, shape, f32) * scale

    def gain(k, shape):
        return 1.0 + 0.05 * jax.random.normal(k, shape, f32)

    L = DEPTH
    dt0 = jnp.exp(jax.random.uniform(ks[9], (L, SSD_HEADS), f32) * (math.log(0.1) - math.log(1e-3)) + math.log(1e-3))
    dt_bias = dt0 + jnp.log(-jnp.expm1(-dt0))
    return {
        "x": jax.random.normal(ks[0], (BATCH, SEQ, D_MODEL), f32),
        "ffn1_norm": gain(ks[1], (L, D_MODEL)),
        "ffn1_w_gate": nrm(ks[2], (L, D_MODEL, D_FF), D_MODEL ** -0.5),
        "ffn1_w_up": nrm(ks[3], (L, D_MODEL, D_FF), D_MODEL ** -0.5),
        "ffn1_w_down": nrm(ks[4], (L, D_FF, D_MODEL), D_FF ** -0.5),
        "mix_norm": gain(ks[5], (L, D_MODEL)),
        "w_in": nrm(ks[6], (L, D_MODEL, IN_DIM), D_MODEL ** -0.5),
        "conv_w": nrm(ks[7], (L, SSD_CONV, CONV_DIM), SSD_CONV ** -0.5),
        "conv_b": nrm(ks[8], (L, CONV_DIM), 0.02),
        "dt_bias": dt_bias,
        "a_log": jnp.log(jax.random.uniform(ks[10], (L, SSD_HEADS), f32, 1.0, 16.0)),
        "d_skip": gain(ks[11], (L, SSD_HEADS)),
        "ssd_norm": gain(ks[12], (L, SSD_DIM)),
        "pool_w": nrm(ks[13], (L, POOL_GROUPS, POOL_GROUP_DIM, POOL_GROUP_DIM), POOL_GROUP_DIM ** -0.5),
        "pool_scale": gain(ks[14], (L, POOL_DIM)),
        "w_out": nrm(ks[15], (L, MIX_DIM, D_MODEL), MIX_DIM ** -0.5),
        "ffn2_norm": gain(ks[16], (L, D_MODEL)),
        "ffn2_w_gate": nrm(ks[17], (L, D_MODEL, D_FF), D_MODEL ** -0.5),
        "ffn2_w_up": nrm(ks[18], (L, D_MODEL, D_FF), D_MODEL ** -0.5),
        "ffn2_w_down": nrm(ks[19], (L, D_FF, D_MODEL), D_FF ** -0.5),
        "final_norm": gain(ks[20], (D_MODEL,)),
    }

def reference(x, ffn1_norm, ffn1_w_gate, ffn1_w_up, ffn1_w_down, mix_norm, w_in, conv_w, conv_b,
              dt_bias, a_log, d_skip, ssd_norm, pool_w, pool_scale, w_out, ffn2_norm,
              ffn2_w_gate, ffn2_w_up, ffn2_w_down, final_norm):
    for i in range(DEPTH):
        x = x + 0.5 * swiglu(rms_norm(x, ffn1_norm[i]), ffn1_w_gate[i], ffn1_w_up[i], ffn1_w_down[i])
        h = rms_norm(x, mix_norm[i])
        proj = h @ w_in[i]
        o1 = SSD_DIM
        o2 = o1 + CONV_DIM
        o3 = o2 + SSD_HEADS
        z, xbc, dt_raw, u = proj[..., :o1], proj[..., o1:o2], proj[..., o2:o3], proj[..., o3:]
        y_ssd = ssd_group(z, xbc, dt_raw, conv_w[i], conv_b[i], dt_bias[i], a_log[i], d_skip[i], ssd_norm[i])
        y_pool = multiscale_pool_group(u, pool_w[i], pool_scale[i])
        x = x + jnp.concatenate([y_ssd, y_pool], axis=-1) @ w_out[i]
        x = x + 0.5 * swiglu(rms_norm(x, ffn2_norm[i]), ffn2_w_gate[i], ffn2_w_up[i], ffn2_w_down[i])
    return rms_norm(x, final_norm)


_drawn_inputs = setup_inputs


def setup_inputs(seed=0):
    import zlib

    import numpy as np

    out = dict(_drawn_inputs(seed))
    spreads = {}
    factors = {'conv_b': 4.047, 'ffn2_norm': 3.817}
    for name, (base, spread) in spreads.items():
        noise = np.random.default_rng([zlib.crc32(name.encode()), seed]).standard_normal(out[name].shape)
        drawn = base * np.exp(spread * noise) if base else spread * noise
        out[name] = __import__('jax').numpy.asarray(drawn.astype(out[name].dtype))
    for name, factor in factors.items():
        out[name] = (out[name] * factor).astype(out[name].dtype)
    return out
```

```python
from contextlib import ExitStack

import numpy as np

import concourse.bass as bass
from concourse import mybir

F32 = mybir.dt.float32
F32R = mybir.dt.float32r
ALU = mybir.AluOpType
ACT = mybir.ActivationFunctionType

P = 128
S = 512
D = 1024
DK = D // P
DFF = 2816
FT = DFF // P
EPS = 1e-6

HEADS = 16
HD = D // HEADS
GROUPS = 2
HG = HEADS // GROUPS
STATE = 128
CH = 128
NC = S // CH
TAPS = 4
CONV = D + 2 * GROUPS * STATE
CT = CONV // P
WINDOWS = (2, 4, 8, 16)
PG = D // len(WINDOWS)
PAD = 16

RING = 4
UB = 8
DOWN = (6, 6, 5, 5)
DOWN0 = (0, 6, 12, 17)

N_GU = 2 * FT
N_DOWN = 4 * DK
M_FFN1 = 0
M_MIX = N_GU + N_DOWN
U_DT = 0
U_CONV = 1
U_Z = U_CONV + CT
U_U = U_Z + DK
U_POOL = U_U + DK
U_OUTP = U_POOL + 2
U_OUTS = U_OUTP + DK
M_FFN2 = M_MIX + U_OUTS + DK
N_UNITS = M_FFN2 + N_GU + N_DOWN

CONV_ORDER = (8, 9, 10, 11, 0, 1, 2, 3, 4, 5, 6, 7)

R_N1, R_MIX, R_N2, R_CW, R_CB = 0, 8, 16, 24, 24 + TAPS * CT
R_SSDN = R_CB + CT
R_PS = R_SSDN + DK
R_ALL = R_PS + DK

SC_DT, SC_ACS, SC_B0, SC_COL, SC_B1, SC_X0 = 0, 1, 2, 3, 4, 5
SC_ST0, SC_X6, SC_ST1, SC_STAT = 11, 14, 16, 19


def sc_x(j):
    return SC_X0 + j if j < 6 else SC_X6 + j - 6


def cols(tile):
    return slice(tile * S, (tile + 1) * S) if isinstance(tile, int) else bass.ds(tile * S, S)


def block(tile):
    return slice(tile * P, (tile + 1) * P) if isinstance(tile, int) else bass.ds(tile * P, P)


def one(i):
    return slice(i, i + 1) if isinstance(i, int) else bass.ds(i, 1)


def build(nc, t, out):
    with ExitStack() as ctx:
        def sb(name, shape, dt=F32):
            return ctx.enter_context(nc.sbuf_tensor(name, shape, dt))

        def sem(name):
            return ctx.enter_context(nc.semaphore(name))

        raw = sb("w_raw", [P, RING, UB, P])
        whi = sb("w_hi_part", [P, RING, UB, P], F32R)
        wlo = sb("w_lo_part", [P, RING, UB, P], F32R)
        xT = sb("xT", [P, DK * S])
        xghi = sb("xghi", [P, DK * S], F32R)
        xglo = sb("xglo", [P, DK * S], F32R)
        rstd = sb("rstd", [P, S])
        sq = sb("sq", [P, S])
        sumsq = sb("sumsq", [P, S])
        ones = sb("ones", [P, P])
        ident = sb("ident", [P, P])
        causal = sb("causal", [P, P])
        prow = sb("prow", [P, P])
        par = sb("par", [P, R_ALL])
        eps = sb("eps", [P, 1])
        inv_count = sb("inv_count", [P, PAD])
        dt_bias = sb("dt_bias", [HEADS, 1])
        a_exp = sb("a_exp", [P, HEADS])
        skip_row = sb("skip_row", [P, HEADS])
        skip_col = sb("skip_col", [P, DK])
        tok_rms = sb("tok_rms", [P, 2, NC])

        base = (nc.sbuf_base + 63) // 64 * 64

        def at(name, offset, shape, dt=F32):
            return nc.alloc_sbuf_tensor_at(name, shape, dt, offset=base + offset)

        KB = 1024
        acthi = at("acthi", 0, [P, FT * S], F32R)
        actlo = at("actlo", 44 * KB, [P, FT * S], F32R)
        xload = at("xload", 88 * KB, [P, 2, D])
        gscaled = xload[:, 0, :].rearrange("p (e s) -> p e s", e=2)
        gsilu = xload[:, 1, :].rearrange("p (e s) -> p e s", e=2)
        gain_out = xload[:, 0, :]
        act32 = at("act32", 96 * KB, [P, 2, S])
        xnew = act32
        xtok = at("xtok", 100 * KB, [P, NC, D])

        xdt = at("xdt", 0, [P, DK, NC, P])
        prev = at("prev", 16 * KB, [P, GROUPS, NC - 1, HG * HD])
        gm = at("gm", 28 * KB, [P, GROUPS, S])
        mixhi = at("mixhi", 0, [P, DK * S], F32R)
        mixlo = at("mixlo", 16 * KB, [P, DK * S], F32R)
        sp0hi = at("sp0hi", 0, [P, 2 * S], F32R)
        sp0lo = at("sp0lo", 4 * KB, [P, 2 * S], F32R)
        xsT = at("xsT", 32 * KB, [P, DK * S])
        zT = at("zT", 48 * KB, [P, DK * S])
        sel32 = at("sel32", 48 * KB, [HEADS, HEADS, P])
        pooled = at("pooled", 64 * KB, [P, DK * S])
        xst = at("xst", 64 * KB, [P, DK // 2, NC - 1, P])
        bT = at("bT", 70 * KB, [P, GROUPS, S])
        btok = at("btok", 74 * KB, [P, GROUPS, S])
        cT = at("cT", 80 * KB, [P, GROUPS, S])
        proj = at("proj", 84 * KB, [P, 2, PAD + S])
        conv = at("conv", 84 * KB + 4224, [P, 2, PAD + S])
        o = 84 * KB + 8448
        ebuf = at("ebuf", o, [P, 2, S])
        cbuf = at("cbuf", o + 4096, [P, 2, S])
        sel = at("sel", o + 8192, [HEADS, HEADS, P], F32R)
        sp1hi = at("sp1hi", o + 8192, [P, 2 * S], F32R)
        sp1lo = at("sp1lo", o + 12288, [P, 2 * S], F32R)
        acsh = at("acsh", o + 16384, [HEADS, S], F32R)
        acsl = at("acsl", o + 18432, [HEADS, S], F32R)
        dtfm = at("dtfm", o + 4096, [HEADS, S])
        acsT = at("acsT", o + 20480, [HEADS, S])
        small = {}
        for i, name in enumerate(("v", "absv", "e", "den", "t", "t2", "q", "dt", "a", "acs", "tot", "wst")):
            small[name] = at("tok_" + name, o + 22528 + 256 * i, [P, NC * HEADS])
        sm = lambda name: small[name][:, :]
        sm3 = lambda name: small[name][:, :].rearrange("p (c h) -> p c h", c=NC)
        assert base + o + 22528 + 256 * 12 <= nc.sbuf_usable_end

        PB = [ctx.enter_context(nc.psum_tensor(f"bank{i}", [P, S], F32)) for i in range(8)]

        landed = [sem(f"landed{i}") for i in range(RING)]
        w_hi, w_lo = sem("w_hi"), sem("w_lo")
        unit_done = sem("unit_done")
        x_landed = [sem(f"x_landed{i}") for i in range(2)]
        par_landed, alog_landed, gain_landed = sem("par_landed"), sem("alog_landed"), sem("gain_landed")
        out_landed = sem("out_landed")
        consts, pool_own = sem("consts"), sem("pool_own")
        x_in, x_ready = sem("x_in"), sem("x_ready")
        par_T, par_ready = sem("par_T"), sem("par_ready")
        xg_hi, xg_lo = sem("xg_hi"), sem("xg_lo")
        sq_own = sem("sq_own")
        stat_ready, std_ready, rstd_ready = sem("stat_ready"), sem("std_ready"), sem("rstd_ready")
        g_scaled, g_silu, g_r = sem("g_scaled"), sem("g_silu"), sem("g_r")
        act_ready, act_hi, act_lo = sem("act_ready"), sem("act_hi"), sem("act_lo")
        proj_read = sem("proj_read")
        pads, sel_made, sel_ready = sem("pads"), sem("sel_made"), sem("sel_ready")
        conv_id, conv_done, silu_done = sem("conv_id"), sem("conv_done"), sem("silu_done")
        scr_ready, scr_read = sem("scr_ready"), sem("scr_read")
        dt_fm_ready, abs_ready, exp_ready, aexp_ready = (
            sem("dt_fm_ready"), sem("abs_ready"), sem("exp_ready"), sem("aexp_ready"))
        a_ready, acs_hi, acs_lo = sem("a_ready"), sem("acs_hi"), sem("acs_lo")
        decay_in, decay_ready = sem("decay_in"), sem("decay_ready")
        g_mm, gm_ready = sem("g_mm"), sem("gm_ready")
        xst_ready, prev_ready = sem("xst_ready"), sem("prev_ready")
        a_bc, d_ready, min_ready, e_ready, ea_ready = (
            sem("a_bc"), sem("d_ready"), sem("min_ready"), sem("e_ready"), sem("ea_ready"))
        m_ready, ce_ready, y_done, y_read = sem("m_ready"), sem("ce_ready"), sem("y_done"), sem("y_read")
        win_ready, pooled_ready = sem("win_ready"), sem("pooled_ready")
        sp_hi, sp_lo, pool_mm, pool_hi, pool_lo = (
            sem("sp_hi"), sem("sp_lo"), sem("pool_mm"), sem("pool_hi"), sem("pool_lo"))
        sz_ready, yg_ready, ysq_ready, ysum_own = sem("sz_ready"), sem("yg_ready"), sem("ysq_ready"), sem("ysum_own")
        grms_ready, grstd_ready, yn_ready = sem("grms_ready"), sem("grstd_ready"), sem("yn_ready")
        mix_hi, mix_lo = sem("mix_hi"), sem("mix_lo")
        tok_ready, tok_read = sem("tok_ready"), sem("tok_read")
        tstat, tstd, trstd, out_ready = sem("tstat"), sem("tstd"), sem("trstd"), sem("out_ready")
        dve_own = sem("dve_own")

        wg = [w[0].rearrange("(k p) f -> p k f", p=P) for w in (t["ffn1_w_gate"], t["ffn2_w_gate"])]
        wu = [w[0].rearrange("(k p) f -> p k f", p=P) for w in (t["ffn1_w_up"], t["ffn2_w_up"])]
        wd = [w[0].rearrange("(k p) f -> p k f", p=P) for w in (t["ffn1_w_down"], t["ffn2_w_down"])]
        w_in = t["w_in"][0].rearrange("(k p) f -> p k f", p=P)
        w_out = t["w_out"][0].rearrange("(k p) f -> p k f", p=P)
        pool_w = t["pool_w"][0].rearrange("g (k p) f -> p (g k) f", p=P)
        Z0, C0, T0, V0 = 0, D, D + CONV, D + CONV + HEADS

        def slot(m):
            return m % RING

        def use(m, i):
            return (m // RING) * 16 + 16 + i * 16

        def pool_output(engine, q):
            if q % 4 == 3:
                engine.wait_ge(unit_done, M_MIX + U_POOL + q // 4 + 1)
            else:
                engine.wait_ge(pool_mm, q + 1 - (q + 1) // 4)

        blk = ctx.enter_context(nc.Block())

        @blk.sync
        def _(sp):
            def fetch(m, i, src, blocks=UB, width=P):
                if not (isinstance(i, int) and m + RING * i < RING):
                    sp.wait_ge(w_hi, i * RING + (m - RING + 1))
                    sp.wait_ge(w_lo, i * RING + (m - RING + 1))
                dst = raw[:, slot(m), 0:blocks, :]
                if width != P:
                    dst = raw[:, slot(m), :, :].rearrange("p (g c) n -> p g (c n)", c=width // P)
                sp.dma_start(dst, src).then_inc(landed[slot(m)], 16)

            def ffn_fetch(f, m0):
                def gate_up(i):
                    for j in range(4):
                        w = (wg, wu)[j % 2][f]
                        c = i * (2 * P) + (j // 2) * P
                        c = slice(c, c + P) if isinstance(c, int) else bass.ds(c, P)
                        fetch(m0 + j, i, w[:, :, c])
                gate_up(0)
                with sp.Fori(1, FT // 2) as i:
                    gate_up(i)
                with sp.Fori(0, DK) as i:
                    for j in range(4):
                        fetch(m0 + N_GU + j, i, wd[f][:, DOWN0[j]:DOWN0[j] + DOWN[j], block(i)], DOWN[j])

            ffn_fetch(0, M_FFN1)
            m = M_MIX
            fetch(m + U_DT, 0, w_in[:, :, T0:T0 + P])
            for i, tile in enumerate(CONV_ORDER):
                fetch(m + U_CONV + i, 0, w_in[:, :, C0 + tile * P:C0 + (tile + 1) * P])
            for i in range(DK):
                fetch(m + U_Z + i, 0, w_in[:, :, Z0 + i * P:Z0 + (i + 1) * P])
            for i in range(DK):
                fetch(m + U_U + i, 0, w_in[:, :, V0 + i * P:V0 + (i + 1) * P])
            for i in range(2):
                fetch(m + U_POOL + i, 0, pool_w[:, 4 * i:4 * i + 4, :], width=PG)
            for i in range(DK):
                fetch(m + U_OUTP + i, 0, w_out[:, DK:2 * DK, block(i)])
            for i in range(DK):
                fetch(m + U_OUTS + i, 0, w_out[:, 0:DK, block(i)])
            ffn_fetch(1, M_FFN2)
            for c in range(NC):
                sp.wait_ge(out_ready, c + 1)
                sp.dma_start(out[0, block(c), :], xtok[:, c, :]).then_inc(out_landed, 16)
            sp.wait_ge(out_landed, 16 * NC)

        @blk.gpsimd
        def _(pool):
            pool.memset(ident[:, :], 0.0).then_inc(pool_own, 1)
            pool.memset(causal[:, :], 1.0).then_inc(pool_own, 1)
            pool.memset(ones[:, :], 1.0).then_inc(consts, 1)
            pool.memset(eps[:, :], EPS).then_inc(consts, 1)
            pool.wait_ge(pool_own, 2)
            pool.affine_select(out=ident[:, :], in_=ident[:, :], compare_op=ALU.not_equal, fill=1.0,
                               base=0, pattern=[[-1, P]], channel_multiplier=1).then_inc(consts, 1)
            pool.affine_select(out=causal[:, :], in_=causal[:, :], compare_op=ALU.is_ge, fill=0.0,
                               base=0, pattern=[[1, P]], channel_multiplier=-1).then_inc(consts, 1)
            for i in range(PAD):
                pool.memset(inv_count[:, i:i + 1], 1.0 / (i + 1)).then_inc(consts, 1)

            def sum_squares(p, source):
                if p:
                    pool.wait_ge(rstd_ready, p)
                pool.memset(sumsq[:, :], 0.0).then_inc(sq_own, 1)

                def tile(d, x):
                    pool.wait_ge(x_ready, d + (DK * p + 1))
                    pool.wait_ge(sq_own, d * 2 + (17 * p + 1))
                    pool.tensor_tensor(sq[:, :], x, x, ALU.mult).then_inc(sq_own, 1)
                    pool.wait_ge(sq_own, d * 2 + (17 * p + 2))
                    pool.tensor_tensor(sumsq[:, :], sumsq[:, :], sq[:, :], ALU.add).then_inc(sq_own, 1)

                if source is xT:
                    with pool.Fori(0, DK) as d:
                        tile(d, xT[:, cols(d)])
                else:
                    with pool.Fori(0, DK // 2) as i:
                        for e in range(2):
                            tile(i * 2 + e, source[:, e, :])

            def gates(f):
                with pool.Fori(0, FT // 2) as i:
                    for e in range(2):
                        pool.wait_ge(g_silu, i * 2 + (FT * f + e + 1))
                        pool.wait_ge(rstd_ready, 1 + 2 * f)
                        pool.tensor_tensor(gsilu[:, e, :], gsilu[:, e, :], rstd[:, :], ALU.mult).then_inc(g_r, 1)

            sum_squares(0, xT)
            gates(0)
            sum_squares(1, xT)

            pool.wait_ge(unit_done, M_MIX)
            pool.memset(proj[:, :, :], 0.0).then_inc(pads, 1)
            pool.memset(conv[:, :, :], 0.0).then_inc(pads, 1)
            pool.memset(sel32[:, :, :], 0.0).then_inc(pool_own, 1)
            pool.wait_ge(pool_own, 3)
            pool.affine_select(out=sel32[:, :, :], in_=sel32[:, :, :], compare_op=ALU.not_equal, fill=1.0,
                               base=0, pattern=[[1, HEADS], [0, P]], channel_multiplier=-1).then_inc(sel_made, 1)

            def state_input(j):
                pool.wait_ge(scr_read, sc_x(j) + 1)
                pool.wait_ge(decay_ready, 1)
                if j >= DK // 2:
                    pool.wait_ge(scr_ready, SC_ST0 + NC - 1)
                w = sm3("wst")[:, 0:NC - 1, 2 * j:2 * j + 2].unsqueeze(3).to_broadcast([P, NC - 1, 2, HD])
                pool.tensor_tensor(
                    xst[:, j % 4, :, :].rearrange("p c (e q) -> p c e q", e=2),
                    xdt[:, j, 0:NC - 1, :].rearrange("p c (e q) -> p c e q", e=2), w, ALU.mult).then_inc(xst_ready, 1)

            def clamp(h):
                pool.wait_ge(d_ready, h + 1)
                pool.tensor_scalar(ebuf[:, h % 2, :], ebuf[:, h % 2, :], 0.0, None, ALU.min).then_inc(min_ready, 1)

            for j in range(6):
                state_input(j)
            clamp(0)
            for h in range(HEADS):
                if h < 2:
                    state_input(6 + h)
                if h + 1 < HEADS:
                    clamp(h + 1)
                if h >= DK:
                    tile = h - DK
                    pool.wait_ge(proj_read, U_U + tile + 1)
                    if tile:
                        pool.wait_ge(pooled_ready, tile)
                    src, shift, b = proj[:, tile % 2, :], 1, 0
                    steps = tile // 2 + 1
                    for s in range(steps):
                        add = pool.tensor_tensor(conv[:, b, PAD:], src[:, PAD:], src[:, PAD - shift:PAD + S - shift], ALU.add)
                        if s < steps - 1:
                            add.then_inc(pool_own, 1)
                            pool.wait_ge(pool_own, 3 + sum(i // 2 for i in range(tile)) + s + 1)
                        else:
                            add.then_inc(win_ready, 1)
                        src, shift, b = conv[:, b, :], 2 * shift, 1 - b
            pool.wait_ge(y_done, HEADS)
            for g in range(GROUPS):
                pool.memset(cbuf[:, g, :], 0.0).then_inc(ysum_own, 1)
            for j in range(DK):
                pool.wait_ge(ysq_ready, j + 1)
                pool.wait_ge(ysum_own, 2 + j)
                pool.tensor_tensor(cbuf[:, j // 4, :], cbuf[:, j // 4, :], ebuf[:, j % 2, :], ALU.add).then_inc(ysum_own, 1)
            for j in range(DK):
                pool.wait_ge(grstd_ready, j // 4 + 1)
                pool.tensor_tensor(xsT[:, cols(j)], xsT[:, cols(j)], cbuf[:, j // 4, :], ALU.mult).then_inc(yn_ready, 1)
            sum_squares(2, xT)
            gates(1)
            sum_squares(3, xnew)

        @blk.scalar
        def _(act):
            def convert(m, i=0):
                act.wait_ge(landed[slot(m)], use(m, i))
                if not (isinstance(i, int) and m + RING * i < RING):
                    act.wait_ge(unit_done, i * RING + (m - RING + 1))
                act.activation(whi[:, slot(m)], raw[:, slot(m)], ACT.Copy).then_inc(w_hi, 1)

            def norm_hi(p, d, gain):
                act.wait_ge(x_ready, d + (DK * p + 1))
                act.activation(xghi[:, cols(d)], xT[:, cols(d)], ACT.Copy,
                               scale=par[:, one(d + gain)]).then_inc(xg_hi, 1)

            def rms(p):
                act.wait_ge(stat_ready, p + 1)
                act.activation(sq[:, :], PB[6][:, :], ACT.Sqrt, bias=eps[:, 0:1], scale=1.0 / D).then_inc(std_ready, 1)

            def gate_up(f, m0, i):
                for j in range(4):
                    e, hidden = j // 2, i * 2 + (FT * f + j // 2)
                    if j % 2 == 0:
                        act.wait_ge(g_scaled, hidden + 1)
                        act.activation(gsilu[:, e, :], gscaled[:, e, :], ACT.Silu).then_inc(g_silu, 1)
                    else:
                        act.wait_ge(act_ready, hidden + 1)
                        act.activation(acthi[:, cols(i * 2 + e)], act32[:, e, :], ACT.Copy).then_inc(act_hi, 1)
                    convert(m0 + j + RING, i)

            for k in range(2):
                act.dma_start(xload[:, k, :], t["x"][0, block(k), :]).then_inc(x_landed[k], 16)
            rows = ((t["ffn1_norm"], R_N1), (t["mix_norm"], R_MIX), (t["ffn2_norm"], R_N2),
                    (t["ssd_norm"], R_SSDN), (t["pool_scale"], R_PS), (t["conv_b"], R_CB))
            for a, r in rows:
                v = a[0].rearrange("(k p) -> k p", p=P)
                act.dma_start(prow[r:r + v.shape[0], :], v).then_inc(par_landed, 16)
            act.dma_start(prow[R_CW:R_CW + TAPS * CT, :],
                          t["conv_w"][0].rearrange("w (k p) -> (w k) p", p=P)).then_inc(par_landed, 16)
            act.dma_start(dt_bias[:, :], t["dt_bias"][0].rearrange("(h a) -> h a", a=1)).then_inc(alog_landed, 16)
            act.dma_start(a_exp[:, :], t["a_log"][0].partition_broadcast(P)).then_inc(alog_landed, 16)
            act.dma_start(skip_row[:, :], t["d_skip"][0].partition_broadcast(P)).then_inc(alog_landed, 16)
            for k in range(2, 4):
                act.wait_ge(x_in, DK * (k - 1))
                act.dma_start(xload[:, k % 2, :], t["x"][0, block(k), :]).then_inc(x_landed[k % 2], 16)
            for m in range(RING):
                convert(m)
            act.wait_ge(par_ready, 1)
            for d in range(DK):
                norm_hi(0, d, R_N1)
            act.wait_ge(consts, 4)
            rms(0)
            gate_up(0, M_FFN1, 0)
            with act.Fori(1, FT // 2) as i:
                gate_up(0, M_FFN1, i)
            with act.Fori(0, DK // 2) as i:
                for e in range(2):
                    for j in range(4):
                        if j == 3:
                            norm_hi(1, i * 2 + e, R_MIX)
                        convert(N_GU + 4 * e + j + RING, i * 2)

            M = M_MIX
            convert(M + U_DT + RING)
            act.wait_ge(sel_made, 1)
            act.activation(sel[:, :, :], sel32[:, :, :], ACT.Copy).then_inc(sel_ready, 1)
            rms(1)
            act.wait_ge(alog_landed, 48)
            act.activation(a_exp[:, :], a_exp[:, :], ACT.Exp).then_inc(aexp_ready, 1)
            for i, tile in enumerate(CONV_ORDER):
                m = U_CONV + i
                act.wait_ge(proj_read, m + 1)
                act.activation(conv[:, i % 2, PAD:], proj[:, i % 2, PAD:], ACT.Identity,
                               bias=par[:, R_CB + tile:R_CB + tile + 1],
                               scale=par[:, R_CW + 3 * CT + tile:R_CW + 3 * CT + tile + 1]).then_inc(conv_id, 1)
                convert(M + m + RING)
                dst = (xsT[:, cols(tile)] if tile < DK else
                       bT[:, tile - DK, :] if tile < DK + GROUPS else cT[:, tile - DK - GROUPS, :])
                act.wait_ge(conv_done, i + 1)
                act.activation(dst, conv[:, i % 2, PAD:], ACT.Silu).then_inc(silu_done, 1)
                if m == 1:
                    act.wait_ge(abs_ready, 1)
                    act.activation(sm("e"), sm("absv"), ACT.Exp, scale=-1.0).then_inc(exp_ready, 1)
                if m == 3:
                    act.wait_ge(scr_read, SC_ACS + 1)
                    act.activation(acsh[:, :], acsT[:, :], ACT.Copy).then_inc(acs_hi, 1)
                if m == 5:
                    act.wait_ge(decay_in, 1)
                    act.activation(sm("wst"), sm("wst"), ACT.Exp).then_inc(decay_ready, 1)
                    act.activation(sm("tot"), sm("tot"), ACT.Exp).then_inc(decay_ready, 1)

            def exps(h):
                act.wait_ge(d_ready, h + 1)
                act.activation(cbuf[:, h % 2, CH:], PB[4 + h % 2][:, CH:], ACT.Exp).then_inc(ea_ready, 1)
                act.wait_ge(min_ready, h + 1)
                act.activation(ebuf[:, h % 2, :], ebuf[:, h % 2, :], ACT.Exp).then_inc(e_ready, 1)

            def split_hi(g):
                if g >= 2:
                    pool_output(act, 2 * g - 3)
                elif g == 1:
                    act.wait_ge(a_bc, HEADS)
                else:
                    act.wait_ge(y_done, DK)
                for k in range(2):
                    act.wait_ge(pooled_ready, 2 * g + k + 1)
                    act.activation((sp0hi, sp1hi)[g % 2][:, cols(k)], pooled[:, cols(2 * g + k)], ACT.Copy).then_inc(sp_hi, 1)

            exps(0)
            for h in range(HEADS):
                convert(M + U_Z + h + RING)
                if h + 1 < HEADS:
                    exps(h + 1)
                if h >= HEADS - 2:
                    split_hi(h - HEADS + 2)
            for g in range(4):
                for d in range(2):
                    q = 2 * g + d
                    pool_output(act, q)
                    act.activation(xghi[:, cols(q)], PB[(U_POOL + q) % 2][:, :], ACT.Copy,
                                   scale=par[:, R_PS + q:R_PS + q + 1]).then_inc(pool_hi, 1)
                if g < 2:
                    split_hi(g + 2)
                if g % 2:
                    convert(M + U_POOL + g // 2 + RING)
            for j in range(DK):
                act.activation(zT[:, cols(j)], zT[:, cols(j)], ACT.Silu).then_inc(sz_ready, 1)
            for j in range(DK):
                act.wait_ge(yg_ready, j + 1)
                if j >= 2:
                    act.wait_ge(ysum_own, 1 + j)
                act.activation(ebuf[:, j % 2, :], xsT[:, cols(j)], ACT.Square).then_inc(ysq_ready, 1)
                if j % 4 == 3:
                    convert(M + U_OUTP + j // 4 + RING)
            convert(M + U_OUTP + 2 + RING)
            convert(M + U_OUTP + 3 + RING)
            for g in range(GROUPS):
                act.wait_ge(scr_ready, SC_STAT + g + 1)
                act.activation(cbuf[:, g, :], PB[2 + (SC_STAT + g) % 2][:, :], ACT.Sqrt,
                               bias=eps[:, 0:1], scale=1.0 / (HG * HD)).then_inc(grms_ready, 1)
            for i in range(4):
                for j in (2 * i, 2 * i + 1):
                    act.wait_ge(yn_ready, j + 1)
                    act.activation(mixhi[:, cols(j)], xsT[:, cols(j)], ACT.Copy,
                                   scale=par[:, R_SSDN + j:R_SSDN + j + 1]).then_inc(mix_hi, 1)
                convert(M + U_OUTP + 4 + i + RING)
            with act.Fori(0, 2) as i:
                for j in range(4):
                    norm_hi(2, i * 4 + j, R_N2)
                    convert(M + U_OUTS + j + RING, i)
            rms(2)
            gate_up(1, M_FFN2, 0)
            with act.Fori(1, FT // 2) as i:
                gate_up(1, M_FFN2, i)
            act.wait_ge(g_silu, 2 * FT)
            act.dma_start(gain_out, t["final_norm"].partition_broadcast(P)).then_inc(gain_landed, 16)
            with act.Fori(0, DK - 1) as i:
                for j in range(4):
                    convert(M_FFN2 + N_GU + j + RING, i)
            act.wait_ge(tstat, 1)
            act.activation(tok_rms[:, 0, :], PB[0][:, 0:NC], ACT.Sqrt, bias=eps[:, 0:1], scale=1.0 / D).then_inc(tstd, 1)
            act.wait_ge(trstd, 1)
            act.wait_ge(tok_read, DK)
            for c in (1, 3):
                act.wait_ge(out_ready, c)
                act.activation(xtok[:, c, :], xtok[:, c, :], ACT.Copy, scale=tok_rms[:, 1, c:c + 1]).then_inc(out_ready, 1)

        @blk.vector
        def _(dve):
            chain = [0]

            def link(ins):
                chain[0] += 1
                ins.then_inc(dve_own, 1)
                dve.wait_ge(dve_own, chain[0])

            def convert(m, i=0):
                dve.wait_ge(w_hi, i * RING + (m + 1))
                dve.tensor_tensor(wlo[:, slot(m)], raw[:, slot(m)], whi[:, slot(m)].bitcast(F32),
                                  ALU.subtract).then_inc(w_lo, 1)

            def norm_lo(p, d, gain):
                dve.wait_ge(xg_hi, d + (DK * p + 1))
                dve.scalar_tensor_tensor(out=xglo[:, cols(d)], in0=xT[:, cols(d)], scalar=par[:, one(d + gain)],
                                         in1=xghi[:, cols(d)].bitcast(F32), op0=ALU.mult,
                                         op1=ALU.subtract).then_inc(xg_lo, 1)

            def inverse(p):
                dve.wait_ge(std_ready, p + 1)
                dve.reciprocal(rstd[:, :], sq[:, :]).then_inc(rstd_ready, 1)
                dve.wait_ge(rstd_ready, p + 1)

            def gate_up(f, m0, i):
                for j in range(4):
                    e, hidden = j // 2, i * 2 + (FT * f + j // 2)
                    dve.wait_ge(unit_done, i * RING + (m0 + j + 1))
                    if j % 2 == 0:
                        dve.tensor_tensor(gscaled[:, e, :], PB[j][:, :], rstd[:, :], ALU.mult).then_inc(g_scaled, 1)
                    else:
                        dve.wait_ge(g_r, hidden + 1)
                        dve.tensor_tensor(act32[:, e, :], PB[j][:, :], gsilu[:, e, :], ALU.mult).then_inc(act_ready, 1)
                        dve.wait_ge(act_hi, hidden + 1)
                        dve.tensor_tensor(actlo[:, cols(i * 2 + e)], act32[:, e, :],
                                          acthi[:, cols(i * 2 + e)].bitcast(F32), ALU.subtract).then_inc(act_lo, 1)
                    convert(m0 + j + RING, i)

            for d in range(DK):
                dve.wait_ge(x_in, 3 * DK + d + 1)
                dve.tensor_copy(xT[:, cols(d)], PB[d][:, :]).then_inc(x_ready, 1)
                if d == 0:
                    dve.wait_ge(par_T, 1)
                    dve.tensor_copy(par[:, :], PB[0][:, 0:R_ALL]).then_inc(par_ready, 1)
            for d in range(DK):
                norm_lo(0, d, R_N1)
                if d % 2:
                    convert(d // 2)
            inverse(0)
            gate_up(0, M_FFN1, 0)
            with dve.Fori(1, FT // 2) as i:
                gate_up(0, M_FFN1, i)

            with dve.Fori(0, DK // 2) as i:
                for e in range(2):
                    for j in range(4):
                        d = i * 2 + e
                        if j == 3:
                            dve.wait_ge(unit_done, i * 8 + (N_GU + 4 * e + 4))
                            dve.scalar_tensor_tensor(out=xT[:, cols(d)], in0=PB[4 + e][:, :], scalar=0.5,
                                                     in1=xT[:, cols(d)], op0=ALU.mult, op1=ALU.add).then_inc(x_ready, 1)
                            norm_lo(1, d, R_MIX)
                        convert(N_GU + 4 * e + j + RING, i * 2)

            M = M_MIX

            def scratch(n):
                dve.wait_ge(scr_ready, n + 1)
                return PB[2 + n % 2]

            def project(q, dst):
                dve.wait_ge(unit_done, M + q + 1)
                rows = dst.shape[0]
                dve.tensor_tensor(dst, PB[q % 2][0:rows, :], rstd[0:rows, :], ALU.mult).then_inc(proj_read, 1)

            def log1p_atanh():
                dve.wait_ge(exp_ready, 1)
                link(dve.tensor_scalar(sm("den"), sm("e"), 2.0, None, ALU.add))
                link(dve.reciprocal(sm("den"), sm("den")))
                link(dve.tensor_tensor(sm("t"), sm("e"), sm("den"), ALU.mult))
                link(dve.tensor_tensor(sm("t2"), sm("t"), sm("t"), ALU.mult))
                link(dve.tensor_scalar(sm("q"), sm("t2"), 1.0 / 17, None, ALU.mult))
                for odd in (15, 13, 11, 9, 7, 5, 3):
                    link(dve.scalar_tensor_tensor(out=sm("q"), in0=sm("q"), scalar=1.0 / odd, in1=sm("t2"),
                                                  op0=ALU.add, op1=ALU.mult))
                link(dve.scalar_tensor_tensor(out=sm("q"), in0=sm("q"), scalar=1.0, in1=sm("t"),
                                              op0=ALU.add, op1=ALU.mult))
                link(dve.tensor_scalar(sm("v"), sm("v"), 0.0, None, ALU.max))
                link(dve.scalar_tensor_tensor(out=sm("dt"), in0=sm("q"), scalar=2.0, in1=sm("v"),
                                              op0=ALU.mult, op1=ALU.add))
                dve.wait_ge(aexp_ready, 1)
                dve.scalar_tensor_tensor(out=sm3("a"), in0=sm3("dt"), scalar=-1.0,
                                         in1=a_exp[:, :].unsqueeze(1).to_broadcast([P, NC, HEADS]),
                                         op0=ALU.mult, op1=ALU.mult).then_inc(a_ready, 1)

            def x_times_dt(j):
                w = sm3("dt")[:, :, 2 * j:2 * j + 2].unsqueeze(3).to_broadcast([P, NC, 2, HD])
                dve.tensor_tensor(xdt[:, j, :, :].rearrange("p c (e q) -> p c e q", e=2),
                                  scratch(sc_x(j))[:, :].rearrange("p (c e q) -> p c e q", c=NC, e=2),
                                  w, ALU.mult).then_inc(scr_read, 1)

            def states(g, first):
                for c in range(NC - 1):
                    bank = scratch(first + c)
                    if c == 0:
                        dve.tensor_copy(prev[:, g, 0, :], bank[:, :]).then_inc(scr_read, 1)
                        dve.wait_ge(scr_read, first + 1)
                        continue
                    dec = sm3("tot")[:, c, HG * g:HG * (g + 1)].unsqueeze(2).to_broadcast([P, HG, HD])
                    view = lambda k: prev[:, g, k, :].rearrange("p (h q) -> p h q", h=HG)
                    link(dve.tensor_tensor(view(c), view(c - 1), dec, ALU.mult))
                    dve.tensor_tensor(prev[:, g, c, :], prev[:, g, c, :], bank[:, :], ALU.add).then_inc(scr_read, 1)
                    dve.wait_ge(scr_read, first + c + 1)

            def difference(h):
                dve.wait_ge(a_bc, h + 1)
                if h >= 2:
                    dve.wait_ge(y_done, h - 1)
                dve.tensor_tensor(ebuf[:, h % 2, :].rearrange("p (c l) -> p c l", c=NC),
                                  PB[4 + h % 2][:, :].rearrange("p (c l) -> p c l", c=NC),
                                  sm3("acs")[:, :, h:h + 1].to_broadcast([P, NC, CH]), ALU.subtract).then_inc(d_ready, 1)

            def weigh(h):
                g = h // HG
                dve.wait_ge(e_ready, h + 1)
                dve.tensor_tensor(ebuf[:, h % 2, :], ebuf[:, h % 2, :], gm[:, g, :], ALU.mult).then_inc(m_ready, 1)
                dve.wait_ge(ea_ready, h + 1)
                dve.tensor_tensor(cbuf[:, h % 2, CH:], cbuf[:, h % 2, CH:], cT[:, g, CH:], ALU.mult).then_inc(ce_ready, 1)

            def skip(p):
                dve.wait_ge(y_done, 2 * p + 2)
                dve.scalar_tensor_tensor(out=xsT[:, cols(p)], in0=xsT[:, cols(p)],
                                         scalar=skip_col[:, p:p + 1], in1=PB[6 + p % 2][:, :],
                                         op0=ALU.mult, op1=ALU.add).then_inc(y_read, 1)

            def pool_mean(j):
                win = WINDOWS[j // 2]
                total = conv[:, (j // 2) % 2, :]
                frame = proj[:, j % 2, :]
                n = win - 1
                dve.wait_ge(win_ready, j + 1)
                dve.scalar_tensor_tensor(out=pooled[:, j * S + n:(j + 1) * S], in0=total[:, PAD + n:], scalar=1.0 / win,
                                         in1=frame[:, PAD + n:], op0=ALU.mult, op1=ALU.subtract)
                head = pooled[:, j * S:j * S + n]
                link(dve.tensor_tensor(head, total[:, PAD:PAD + n], inv_count[:, 0:n], ALU.mult))
                dve.tensor_tensor(head, head, frame[:, PAD:PAD + n], ALU.subtract).then_inc(pooled_ready, 1)

            def split_lo(g):
                for k in range(2):
                    dve.wait_ge(sp_hi, 2 * g + k + 1)
                    dve.tensor_tensor((sp0lo, sp1lo)[g % 2][:, cols(k)], pooled[:, cols(2 * g + k)],
                                      (sp0hi, sp1hi)[g % 2][:, cols(k)].bitcast(F32), ALU.subtract).then_inc(sp_lo, 1)

            convert(M + U_DT + RING)
            inverse(1)
            project(U_DT, dtfm[:, :])
            dve.wait_ge(proj_read, 1)
            dve.wait_ge(alog_landed, 48)
            dve.tensor_scalar(dtfm[:, :], dtfm[:, :], dt_bias[:, 0:1], None, ALU.add).then_inc(dt_fm_ready, 1)
            pairs = skip_row[:, :].rearrange("p (j e) -> p j e", e=2)
            for e in range(2):
                half = slice(e * HD, (e + 1) * HD)
                link(dve.tensor_copy(skip_col[half, :], pairs[half, :, e]))
            dve.wait_ge(pads, 2)
            dve.wait_ge(consts, 4 + PAD)
            for i, tile in enumerate(CONV_ORDER):
                m = U_CONV + i
                project(m, proj[:, i % 2, PAD:])
                dve.wait_ge(conv_id, i + 1)
                for tap in range(TAPS - 1):
                    back = TAPS - 1 - tap
                    r = R_CW + tap * CT + tile
                    stt = dve.scalar_tensor_tensor(
                        out=conv[:, i % 2, PAD:], in0=proj[:, i % 2, PAD - back:PAD + S - back], scalar=par[:, r:r + 1],
                        in1=conv[:, i % 2, PAD:], op0=ALU.mult, op1=ALU.add)
                    if tap < TAPS - 2:
                        link(stt)
                    else:
                        stt.then_inc(conv_done, 1)
                convert(M + m + RING)
                if m == 1:
                    dve.tensor_copy(sm("v"), scratch(SC_DT)[:, 0:NC * HEADS]).then_inc(scr_read, 1)
                    dve.wait_ge(scr_read, SC_DT + 1)
                    dve.scalar_tensor_tensor(out=sm("absv"), in0=sm("v"), scalar=-1.0, in1=sm("v"),
                                             op0=ALU.mult, op1=ALU.max).then_inc(abs_ready, 1)
                if m == 2:
                    log1p_atanh()
                if m == 3:
                    dve.tensor_copy(acsT[:, :], scratch(SC_ACS)[0:HEADS, :]).then_inc(scr_read, 1)
                if m == 4:
                    dve.wait_ge(acs_hi, 1)
                    dve.tensor_tensor(acsl[:, :], acsT[:, :], acsh[:, :].bitcast(F32), ALU.subtract).then_inc(acs_lo, 1)
                    dve.tensor_copy(btok[:, 0, :], scratch(SC_B0)[:, :]).then_inc(scr_read, 1)
                if m == 5:
                    bank = scratch(SC_COL)
                    link(dve.tensor_copy(sm("acs"), bank[:, 64:128]))
                    dve.tensor_copy(sm("tot"), bank[:, 0:64]).then_inc(scr_read, 1)
                    dve.wait_ge(scr_read, SC_COL + 1)
                    link(dve.tensor_tensor(sm("wst"), sm("tot"), sm("acs"), ALU.subtract))
                    dve.tensor_scalar(sm("wst"), sm("wst"), 0.0, None, ALU.min).then_inc(decay_in, 1)
                if m == 6:
                    dve.tensor_copy(btok[:, 1, :], scratch(SC_B1)[:, :]).then_inc(scr_read, 1)
                    for g in range(GROUPS):
                        dve.wait_ge(g_mm, g + 1)
                        dve.tensor_tensor(gm[:, g, :].rearrange("p (c l) -> p c l", c=NC),
                                          PB[4 + g][:, :].rearrange("p (c l) -> p c l", c=NC),
                                          causal[:, :].unsqueeze(1).to_broadcast([P, NC, CH]), ALU.mult).then_inc(gm_ready, 1)
                if m >= 7:
                    x_times_dt(m - 7)
            dve.wait_ge(decay_ready, 2)
            states(0, SC_ST0)
            difference(0)
            for h in range(HEADS):
                m = U_Z + h
                weigh(h)
                if h == 4:
                    states(1, SC_ST1)
                if h >= 2 and h % 2 == 0:
                    skip(h // 2 - 1)
                if h < DK:
                    project(m, zT[:, cols(h)])
                else:
                    u = h - DK
                    dve.wait_ge(unit_done, M + m + 1)
                    if u >= 2:
                        dve.wait_ge(pooled_ready, u - 1)
                    dve.tensor_tensor(proj[:, u % 2, PAD:], PB[m % 2][:, :], rstd[:, :], ALU.mult).then_inc(proj_read, 1)
                if h < 2:
                    x_times_dt(6 + h)
                if h + 1 < HEADS:
                    difference(h + 1)
                convert(M + m + RING)
                if h > DK:
                    pool_mean(h - DK - 1)
                if h >= HEADS - 2:
                    split_lo(h - HEADS + 2)
            pool_mean(DK - 1)
            skip(DK - 1)
            for g in range(4):
                for d in range(2):
                    q = 2 * g + d
                    dve.wait_ge(pool_hi, q + 1)
                    dve.scalar_tensor_tensor(out=xglo[:, cols(q)], in0=PB[(U_POOL + q) % 2][:, :],
                                             scalar=par[:, R_PS + q:R_PS + q + 1], in1=xghi[:, cols(q)].bitcast(F32),
                                             op0=ALU.mult, op1=ALU.subtract).then_inc(pool_lo, 1)
                if g < 2:
                    split_lo(g + 2)
                if g % 2:
                    convert(M + U_POOL + g // 2 + RING)
            for j in range(DK):
                dve.wait_ge(sz_ready, j + 1)
                dve.tensor_tensor(xsT[:, cols(j)], xsT[:, cols(j)], zT[:, cols(j)], ALU.mult).then_inc(yg_ready, 1)
            for d in range(DK):
                dve.wait_ge(unit_done, M + U_OUTP + d + 1)
                dve.tensor_tensor(xT[:, cols(d)], PB[(U_OUTP + d) % 2][:, :], xT[:, cols(d)], ALU.add).then_inc(proj_read, 1)
                if d >= 4:
                    for j in (2 * (d - 4), 2 * (d - 4) + 1):
                        dve.wait_ge(mix_hi, j + 1)
                        dve.scalar_tensor_tensor(out=mixlo[:, cols(j)], in0=xsT[:, cols(j)],
                                                 scalar=par[:, R_SSDN + j:R_SSDN + j + 1],
                                                 in1=mixhi[:, cols(j)].bitcast(F32),
                                                 op0=ALU.mult, op1=ALU.subtract).then_inc(mix_lo, 1)
                convert(M + U_OUTP + d + RING)
                if d == 3:
                    for g in range(GROUPS):
                        dve.wait_ge(grms_ready, g + 1)
                        dve.reciprocal(cbuf[:, g, :], cbuf[:, g, :]).then_inc(grstd_ready, 1)
            with dve.Fori(0, 2) as i:
                for j in range(4):
                    d = i * 4 + j
                    dve.wait_ge(unit_done, d + (M + U_OUTS + 1))
                    dve.tensor_tensor(xT[:, cols(d)], PB[4 + j % 2][:, :], xT[:, cols(d)], ALU.add).then_inc(x_ready, 1)
                    norm_lo(2, d, R_N2)
                    convert(M + U_OUTS + j + RING, i)
            inverse(2)
            gate_up(1, M_FFN2, 0)
            with dve.Fori(1, FT // 2) as i:
                gate_up(1, M_FFN2, i)

            def tokens(d):
                dve.wait_ge(tok_ready, d + 1)
                bank = PB[6 + d % 2] if isinstance(d, int) else PB[6 + d_parity[0]]
                dve.tensor_tensor(xtok[:, :, block(d)], bank[:, :].rearrange("p (c f) -> p c f", c=NC),
                                  gain_out[:, block(d)].unsqueeze(1).to_broadcast([P, NC, P]), ALU.mult).then_inc(tok_read, 1)

            d_parity = [0]

            def down(i, last=False):
                for e in range(2):
                    d = i * 2 + e
                    for j in range(4):
                        m = N_GU + 4 * e + j
                        if j == 1 and not (isinstance(i, int) and i == 0 and e == 0):
                            d_parity[0] = 1 - e
                            tokens(d - 1)
                        if j == 3:
                            dve.wait_ge(unit_done, i * 8 + (M_FFN2 + m + 1))
                            if not (isinstance(i, int) and i == 0):
                                dve.wait_ge(sq_own, d * 2 + (17 * 3 - 2))
                            dve.scalar_tensor_tensor(out=xnew[:, e, :], in0=PB[4 + e][:, :], scalar=0.5,
                                                     in1=xT[:, cols(d)], op0=ALU.mult, op1=ALU.add).then_inc(x_ready, 1)
                        if not (last and e == 1):
                            convert(M_FFN2 + m + RING, i * 2)

            dve.wait_ge(gain_landed, 16)
            down(0)
            with dve.Fori(1, DK // 2 - 1) as i:
                down(i)
            down(DK // 2 - 1, last=True)
            tokens(DK - 1)
            dve.wait_ge(tstd, 1)
            dve.reciprocal(tok_rms[:, 1, :], tok_rms[:, 0, :]).then_inc(trstd, 1)
            dve.wait_ge(trstd, 1)
            dve.wait_ge(tok_read, DK)
            for c in (0, 2):
                if c:
                    dve.wait_ge(out_ready, c)
                dve.tensor_scalar(xtok[:, c, :], xtok[:, c, :], tok_rms[:, 1, c:c + 1], None, ALU.mult).then_inc(out_ready, 1)

        @blk.tensor
        def _(pe):
            def products(bank, m, i, blocks, hi, lo, k0, first=True, last=True, ready=None):
                pe.wait_ge(w_hi, i * RING + (m + 1))
                pe.wait_ge(w_lo, i * RING + (m + 1))
                s = slot(m)
                for k in range(blocks):
                    if ready:
                        pe.wait_ge(ready[0], ready[1] + k + 1)
                    h, l = hi[:, cols(k0 + k)], lo[:, cols(k0 + k)]
                    pe.matmul(bank, whi[:, s, k, :], h, start=first and k == 0, stop=False)
                    pe.matmul(bank, whi[:, s, k, :], l, start=False, stop=False)
                    mm = pe.matmul(bank, wlo[:, s, k, :], h, start=False, stop=last and k == blocks - 1)
                mm.then_inc(unit_done, 1)

            def stat(p):
                pe.wait_ge(sq_own, 17 * (p + 1))
                pe.matmul(PB[6][:, :], ones[:, :], sumsq[:, :], start=True, stop=True).then_inc(stat_ready, 1)

            def gate_up(f, m0, i):
                first = isinstance(i, int)
                for j in range(4):
                    if not first:
                        pe.wait_ge((g_scaled, act_ready)[j % 2], i * 2 + (FT * f + j // 2 - 1))
                    elif j == 0:
                        pe.wait_ge(x_ready, DK * 2 * f + 1)
                    products(PB[j][:, :], m0 + j, i, UB, xghi, xglo, 0,
                             ready=(xg_lo, DK * 2 * f) if first and j == 0 else None)
                    if first and j == 0:
                        stat(2 * f)

            def down(f, m0, i, behind=None):
                for e in range(2):
                    d = i * 2 + e
                    for j in range(4):
                        if j == 0:
                            if isinstance(i, int) and i == 0:
                                pe.wait_ge(x_ready, DK * (2 * f + 1))
                            else:
                                pe.wait_ge(x_ready, d + (DK * (2 * f + 1) - 1))
                        pe.wait_ge(act_lo, FT * f + DOWN0[j] + DOWN[j])
                        products(PB[4 + e][:, :], m0 + N_GU + 4 * e + j, i * 2, DOWN[j], acthi, actlo, DOWN0[j],
                                 first=j == 0, last=j == 3)
                        if j == 0 and behind and not (isinstance(i, int) and i == 0 and e == 0):
                            behind(d - 1, 1 - e)

            pe.wait_ge(consts, 4)
            for c in range(NC):
                pe.wait_ge(x_landed[c % 2], 16 * (c // 2 + 1))
                for d in range(DK):
                    pe.transpose(PB[d][:, block(c)], xload[:, c % 2, block(d)], ident[:, :]).then_inc(x_in, 1)
            pe.wait_ge(par_landed, 16 * 7)
            pe.wait_ge(x_ready, 1)
            pe.transpose(PB[0][:, 0:R_ALL], prow[0:R_ALL, :], ident[0:R_ALL, 0:R_ALL]).then_inc(par_T, 1)
            pe.wait_ge(par_ready, 1)
            pe.wait_ge(x_ready, DK)

            gate_up(0, M_FFN1, 0)
            with pe.Fori(1, FT // 2) as i:
                gate_up(0, M_FFN1, i)
            down(0, M_FFN1, 0)
            with pe.Fori(1, DK // 2) as i:
                down(0, M_FFN1, i)

            M = M_MIX

            def scratch(n):
                if n >= 2:
                    pe.wait_ge(scr_read, n - 1)
                return PB[2 + n % 2]

            def project(m, ready=None):
                if m >= 2:
                    pe.wait_ge(proj_read, m - 1)
                products(PB[m % 2][:, :], M + m, 0, UB, xghi, xglo, 0, ready=ready)

            def chunks_to_tokens(bank, src, width=P, off=0, rows=P):
                for c in range(NC):
                    mm = pe.transpose(bank[:, off + c * width:off + (c + 1) * width], src[:, block(c)],
                                      ident[0:rows, 0:rows])
                return mm

            def x_to_tokens(j):
                pe.wait_ge(silu_done, 4 + j + 1)
                chunks_to_tokens(scratch(sc_x(j)), xsT[:, cols(j)]).then_inc(scr_ready, 1)

            def state_products(g, first):
                pe.wait_ge(xst_ready, 4 * (g + 1))
                for c in range(NC - 1):
                    pe.matmul(scratch(first + c)[:, :].rearrange("p (j f) -> p j f", j=4), btok[:, g, block(c)],
                              xst[:, :, c, :], start=True, stop=True).then_inc(scr_ready, 1)

            def decay_rows(h):
                if h < 2:
                    pe.wait_ge(gm_ready, h + 1)
                else:
                    pe.wait_ge(ea_ready, h - 1)
                pe.matmul(PB[4 + h % 2][:, :], sel[:, h, :], acsh[:, :], start=True, stop=False)
                pe.matmul(PB[4 + h % 2][:, :], sel[:, h, :], acsl[:, :], start=False, stop=True).then_inc(a_bc, 1)

            def scan(h):
                g, tile, lo = h // HG, h // 2, (h % 2) * HD
                if h % 2 == 0 and tile >= 2:
                    pe.wait_ge(y_read, tile - 1)
                pe.wait_ge(m_ready, h + 1)
                pe.wait_ge(ce_ready, h + 1)
                for c in range(NC):
                    dst = PB[6 + tile % 2][lo:lo + HD, block(c)]
                    mm = pe.matmul(dst, xdt[:, tile, c, lo:lo + HD], ebuf[:, h % 2, block(c)], start=True, stop=c == 0)
                    if c:
                        q = (h % HG) * HD
                        mm = pe.matmul(dst, prev[:, g, c - 1, q:q + HD], cbuf[:, h % 2, block(c)], start=False, stop=True)
                mm.then_inc(y_done, 1)

            project(U_DT, ready=(xg_lo, DK))
            stat(1)
            for i in range(CT):
                m = U_CONV + i
                project(m)
                if m == 1:
                    pe.wait_ge(dt_fm_ready, 1)
                    chunks_to_tokens(scratch(SC_DT), dtfm, width=HEADS, rows=HEADS).then_inc(scr_ready, 1)
                if m == 3:
                    pe.wait_ge(a_ready, 1)
                    bank = scratch(SC_ACS)
                    for c in range(NC):
                        mm = pe.matmul(bank[0:HEADS, block(c)], sm3("a")[:, c, :], causal[:, :], start=True, stop=True)
                    mm.then_inc(scr_ready, 1)
                if m == 4:
                    pe.wait_ge(silu_done, 1)
                    chunks_to_tokens(scratch(SC_B0), bT[:, 0, :]).then_inc(scr_ready, 1)
                if m == 5:
                    pe.wait_ge(scr_read, SC_ACS + 1)
                    bank = scratch(SC_COL)
                    pe.matmul(bank[:, 0:NC * HEADS], ones[:, :], sm("a"), start=True, stop=True)
                    chunks_to_tokens(bank, acsT, width=HEADS, off=NC * HEADS, rows=HEADS).then_inc(scr_ready, 1)
                if m == 6:
                    pe.wait_ge(silu_done, 4)
                    chunks_to_tokens(scratch(SC_B1), bT[:, 1, :]).then_inc(scr_ready, 1)
                    for g in range(GROUPS):
                        for c in range(NC):
                            mm = pe.matmul(PB[4 + g][:, block(c)], bT[:, g, block(c)], cT[:, g, block(c)],
                                           start=True, stop=True)
                        mm.then_inc(g_mm, 1)
                if m >= 7:
                    x_to_tokens(m - 7)
            state_products(0, SC_ST0)
            pe.wait_ge(acs_lo, 1)
            pe.wait_ge(sel_ready, 1)
            decay_rows(0)
            for h in range(HEADS):
                project(U_Z + h)
                if h < 2:
                    x_to_tokens(6 + h)
                if h + 1 < HEADS:
                    decay_rows(h + 1)
                scan(h)
                if h == 3:
                    state_products(1, SC_ST1)
            for g in range(4):
                m = M + U_POOL + g // 2
                if g % 2 == 0:
                    pe.wait_ge(w_hi, m + 1)
                    pe.wait_ge(w_lo, m + 1)
                pe.wait_ge(sp_lo, 2 * g + 2)
                hi, lo = ((sp0hi, sp0lo), (sp1hi, sp1lo))[g % 2]
                for d in range(2):
                    q = 2 * g + d
                    pe.wait_ge(proj_read, min(U_POOL, U_POOL + q - 1))
                    if q >= 2:
                        pe.wait_ge(pool_lo, q - 1)
                    bank = PB[(U_POOL + q) % 2][:, :]
                    for k in range(2):
                        b = (g % 2) * 4 + 2 * k + d
                        pe.matmul(bank, whi[:, slot(m), b, :], hi[:, cols(k)], start=k == 0, stop=False)
                        pe.matmul(bank, whi[:, slot(m), b, :], lo[:, cols(k)], start=False, stop=False)
                        mm = pe.matmul(bank, wlo[:, slot(m), b, :], hi[:, cols(k)], start=False, stop=k == 1)
                    mm.then_inc(unit_done if q % 4 == 3 else pool_mm, 1)
            for d in range(DK):
                if d == 0:
                    pe.wait_ge(pool_lo, DK - 1)
                if d >= 2:
                    pe.wait_ge(proj_read, U_POOL + d - 1)
                products(PB[(U_OUTP + d) % 2][:, :], M + U_OUTP + d, 0, UB, xghi, xglo, 0,
                         ready=(pool_lo, 0) if d == 0 else None)
                if d == 3:
                    for g in range(GROUPS):
                        pe.wait_ge(ysum_own, 2 + 4 * (g + 1))
                        pe.matmul(scratch(SC_STAT + g)[:, :], ones[:, :], cbuf[:, g, :],
                                  start=True, stop=True).then_inc(scr_ready, 1)
            pe.wait_ge(mix_lo, DK)
            with pe.Fori(0, 2) as i:
                for j in range(4):
                    d = i * 4 + j
                    pe.wait_ge(x_ready, d + (2 * DK - 1))
                    products(PB[4 + j % 2][:, :], M + U_OUTS + j, i, UB, mixhi, mixlo, 0)
            gate_up(1, M_FFN2, 0)
            with pe.Fori(1, FT // 2) as i:
                gate_up(1, M_FFN2, i)

            def to_tokens(d, e):
                pe.wait_ge(x_ready, d + (3 * DK + 1))
                if not (isinstance(d, int) and d < 2):
                    pe.wait_ge(tok_read, d - 1)
                for c in range(NC):
                    mm = pe.transpose(PB[6 + e][:, block(c)], xnew[:, e, block(c)], ident[:, :])
                mm.then_inc(tok_ready, 1)

            down(1, M_FFN2, 0, to_tokens)
            with pe.Fori(1, DK // 2) as i:
                down(1, M_FFN2, i, to_tokens)
            to_tokens(DK - 1, 1)
            pe.wait_ge(sq_own, 17 * 4)
            for c in range(NC):
                mm = pe.matmul(PB[0][:, c:c + 1], sumsq[:, block(c)], ones[:, 0:1], start=True, stop=True)
            mm.then_inc(tstat, 1)


_INS = ["x", "ffn1_norm", "ffn1_w_gate", "ffn1_w_up", "ffn1_w_down", "mix_norm", "w_in", "conv_w", "conv_b",
        "dt_bias", "a_log", "d_skip", "ssd_norm", "pool_w", "pool_scale", "w_out", "ffn2_norm",
        "ffn2_w_gate", "ffn2_w_up", "ffn2_w_down", "final_norm"]


def kernel(**inputs):
    import concourse.bacc as bacc
    from concourse.bass_utils import run_bass_kernel_spmd

    nc = bacc.Bacc("TRN2", target_bir_lowering=False, num_devices=1, dynamic_dma_scratch_size=1024)
    arrays, aps = {}, {}
    for name in _INS:
        a = np.ascontiguousarray(inputs[name])
        arrays["in_" + name] = a
        aps[name] = nc.dram_tensor("in_" + name, a.shape, mybir.dt.from_np(a.dtype), kind="ExternalInput").ap()
    out = nc.dram_tensor("out", (1, S, D), F32, kind="ExternalOutput").ap()
    build(nc, aps, out)
    return run_bass_kernel_spmd(nc, [arrays], core_ids=[0]).results[0]["out"]
```

```python
from contextlib import ExitStack

import numpy as np

import concourse.bass as bass
from concourse import mybir

F32 = mybir.dt.float32
F32R = mybir.dt.float32r
ALU = mybir.AluOpType
ACT = mybir.ActivationFunctionType

P = 128
S = 512
D = 1024
DK = D // P
DFF = 2816
FT = DFF // P
EPS = 1e-6

HEADS = 16
HD = D // HEADS
GROUPS = 2
HG = HEADS // GROUPS
LOW = 32
SPLIT = LOW + HEADS
STATE = 128
CH = 128
NC = S // CH
HALF = S // 2
TAPS = 4
CONV = D + 2 * GROUPS * STATE
CT = CONV // P
WINDOWS = (2, 4, 8, 16)
PG = D // len(WINDOWS)
PAD = 16

RING = 4
UB = 8
DOWN = (6, 6, 5, 5)
DOWN0 = (0, 6, 12, 17)

LAST_BANK, LAST_TOKENS, LAST_STAT = (5, 1), (7, 3), (0, 2)

N_GU = 2 * FT
N_DOWN = 4 * DK
M_FFN1 = 0
M_MIX = N_GU + N_DOWN
U_DT = 0
U_CONV = 1
U_Z = U_CONV + CT
U_U = U_Z + DK
U_POOL = U_U + DK
U_OUTP = U_POOL + 2
U_OUTS = U_OUTP + DK
M_FFN2 = M_MIX + U_OUTS + DK
N_UNITS = M_FFN2 + N_GU + N_DOWN

CONV_ORDER = (8, 9, 10, 11, 0, 1, 2, 3, 4, 5, 6, 7)

R_N1, R_MIX, R_N2, R_CW, R_CB = 0, 8, 16, 24, 24 + TAPS * CT
R_SSDN = R_CB + CT
R_PS = R_SSDN + DK
R_ALL = R_PS + DK

POOL_BANKS = (1, 0, 2, 3, 4, 5, 6, 7)

SCRATCH = ("dt", "b0", "b1", "acs", "col", "x0", "x1", "x2", "x3", "state00", "state01", "state02",
           "x4", "x5", "x6", "x7", "state10", "state11", "state12", "stat0", "stat1")
SC = {name: i for i, name in enumerate(SCRATCH)}

U_ORDER = (6, 7, 4, 5, 2, 3, 0, 1)
SPLIT_AT = (12, 14, 15)


def cols(tile):
    return slice(tile * S, (tile + 1) * S) if isinstance(tile, int) else bass.ds(tile * S, S)


def block(tile):
    return slice(tile * P, (tile + 1) * P) if isinstance(tile, int) else bass.ds(tile * P, P)


def one(i):
    return slice(i, i + 1) if isinstance(i, int) else bass.ds(i, 1)


def build(nc, t, out):
    with ExitStack() as ctx:
        def sb(name, shape, dt=F32):
            return ctx.enter_context(nc.sbuf_tensor(name, shape, dt))

        def sem(name):
            return ctx.enter_context(nc.semaphore(name))

        raw = sb("w_raw", [P, RING, UB, P])
        whi = sb("w_hi_part", [P, RING, UB, P], F32R)
        wlo = sb("w_lo_part", [P, RING, UB, P], F32R)
        xT = sb("xT", [P, DK * S])
        xghi = sb("xghi", [P, DK * S], F32R)
        xglo = sb("xglo", [P, DK * S], F32R)
        rstd = sb("rstd", [P, S])
        sq = sb("sq", [P, 2, S])
        sumsq = sb("sumsq", [P, S])
        ones = sb("ones", [P, P])
        ident = sb("ident", [P, P])
        causal = sb("causal", [P, P])
        par = sb("par", [P, R_ALL])
        eps = sb("eps", [P, 1])
        inv_count = sb("inv_count", [P, PAD])
        dt_bias = sb("dt_bias", [HEADS, 1])
        a_exp = sb("a_exp", [P, HEADS])
        skip_row = sb("skip_row", [P, HEADS])
        skip_col = sb("skip_col", [P, DK])
        tok_rms = sb("tok_rms", [P, 2, NC])

        base = (nc.sbuf_base + 63) // 64 * 64

        def at(name, offset, shape, dt=F32):
            return nc.alloc_sbuf_tensor_at(name, shape, dt, offset=base + offset)

        KB = 1024
        acthi = at("acthi", 0, [P, FT * S], F32R)
        actlo = at("actlo", 44 * KB, [P, FT * S], F32R)
        xload = at("xload", 0, [P, NC, D])
        prow = at("prow", 16 * KB, [P, P])
        gate_buf = at("gate_buf", 88 * KB, [P, 2, D])
        gscaled = gate_buf[:, 0, :].rearrange("p (e s) -> p e s", e=2)
        gsilu = gate_buf[:, 1, :].rearrange("p (e s) -> p e s", e=2)
        gain_out = gate_buf[:, 0, :]
        act32 = at("act32", 96 * KB, [P, 2, S])
        xnew = act32
        xtok = at("xtok", 100 * KB, [P, NC, D])

        xdt = at("xdt", 0, [P, DK, NC, P])
        prev = at("prev", 16 * KB, [P, GROUPS, NC - 1, HG * HD])
        gm = at("gm", 28 * KB, [P, GROUPS, S])
        mixhi = at("mixhi", 0, [P, DK * S], F32R)
        mixlo = at("mixlo", 16 * KB, [P, DK * S], F32R)
        sp0 = [[at(f"sp0{n}{k}", (4 * i + 2 * k) * KB, [P, S], F32R) for k in range(2)] for i, n in enumerate("hl")]
        sp1 = [[at("sp1h0", 16 * KB, [P, S], F32R), at("sp1h1", 18 * KB, [P, S], F32R)],
               [at("sp1l0", 20 * KB, [P, S], F32R), at("sp1l1", 28 * KB, [P, S], F32R)]]
        xsT = at("xsT", 32 * KB, [P, DK * S])
        zT = at("zT", 48 * KB, [P, DK * S])
        sel32 = at("sel32", 48 * KB, [SPLIT, HEADS, P])
        pooled = at("pooled", 64 * KB, [P, DK * S])
        xst = at("xst", 64 * KB, [P, DK // 2, NC - 1, P])
        bT = at("bT", 70 * KB, [P, GROUPS, S])
        btok = at("btok", 74 * KB, [P, GROUPS, S])
        cT = at("cT", 80 * KB, [P, GROUPS, S])
        proj = at("proj", 84 * KB, [P, 2, PAD + S])
        conv = at("conv", 84 * KB + 4224, [P, 2, PAD + S])
        o = 84 * KB + 8448
        ebuf = at("ebuf", o, [P, 2, S])
        cbuf = at("cbuf", o + 4096, [P, 2, S])
        sel = at("sel", o + 8192, [SPLIT, HEADS, P], F32R)
        sp2 = [[at(f"sp2{n}{k}", o + 8192 + 2048 * (2 * i + k), [P, S], F32R) for k in range(2)]
               for i, n in enumerate("hl")]
        splits = (sp0, sp1, sp2, sp0)
        acs_split = at("acs_split", o + 16384, [SPLIT, S], F32R)
        dtfm = at("dtfm", o + 4096, [HEADS, S])
        acsT = at("acsT", o + 6144, [SPLIT, S])
        small = {}
        for i, name in enumerate(("v", "absv", "e", "den", "t", "t2", "q", "dt", "acs", "tot", "wst")):
            small[name] = at("tok_" + name, o + 18432 + 256 * i, [P, NC * HEADS])
        a2 = at("tok_a", o + 18432 + 256 * len(small), [P, NC, SPLIT])
        sm = lambda name: small[name][:, :]
        sm3 = lambda name: small[name][:, :].rearrange("p (c h) -> p c h", c=NC)
        assert base + o + 18432 + 256 * len(small) + 4 * NC * SPLIT <= nc.sbuf_usable_end

        PB = [ctx.enter_context(nc.psum_tensor(f"bank{i}", [P, S], F32)) for i in range(8)]

        landed = [sem(f"landed{i}") for i in range(RING)]
        w_hi, w_lo = sem("w_hi"), sem("w_lo")
        unit_done = sem("unit_done")
        x_landed = [sem(f"x_landed{i}") for i in range(NC)]
        par_landed, alog_landed, gain_landed = sem("par_landed"), sem("alog_landed"), sem("gain_landed")
        out_landed = sem("out_landed")
        consts, pool_own = sem("consts"), sem("pool_own")
        x_in, x_moved, x_ready = sem("x_in"), sem("x_moved"), sem("x_ready")
        par_T, par_ready = sem("par_T"), sem("par_ready")
        xg_hi, xg_lo = sem("xg_hi"), sem("xg_lo")
        sq_ready, sum_own = sem("sq_ready"), sem("sum_own")
        stat_ready, std_ready, rstd_ready = sem("stat_ready"), sem("std_ready"), sem("rstd_ready")
        g_scaled, g_silu, g_r = sem("g_scaled"), sem("g_silu"), sem("g_r")
        act_ready, act_hi, act_lo = sem("act_ready"), sem("act_hi"), sem("act_lo")
        proj_read = sem("proj_read")
        pads, sel_made, sel_ready = sem("pads"), sem("sel_made"), sem("sel_ready")
        conv_id, tap_ready, conv_done, conv_sum, silu_done = (
            sem("conv_id"), sem("tap_ready"), sem("conv_done"), sem("conv_sum"), sem("silu_done"))
        scr_ready, scr_read = sem("scr_ready"), sem("scr_read")
        dt_fm_ready, abs_ready, exp_ready, aexp_ready = (
            sem("dt_fm_ready"), sem("abs_ready"), sem("exp_ready"), sem("aexp_ready"))
        a_ready, acs_hi, acs_lo = sem("a_ready"), sem("acs_hi"), sem("acs_lo")
        decay_in, decay_ready = sem("decay_in"), sem("decay_ready")
        g_mm, gm_ready = sem("g_mm"), sem("gm_ready")
        xst_ready, prev_ready = sem("xst_ready"), sem("prev_ready")
        a_bc, d_ready, min_ready, e_ready, ea_ready = (
            sem("a_bc"), sem("d_ready"), sem("min_ready"), sem("e_ready"), sem("ea_ready"))
        m_ready, ce_ready, y_done, y_read = sem("m_ready"), sem("ce_ready"), sem("y_done"), sem("y_read")
        win_ready, pooled_ready = sem("win_ready"), sem("pooled_ready")
        sp_hi, sp_lo, pool_mm, pool_hi, pool_lo = (
            sem("sp_hi"), sem("sp_lo"), sem("pool_mm"), sem("pool_hi"), sem("pool_lo"))
        sz_ready, yg_ready, ysq_ready, ysum_own = sem("sz_ready"), sem("yg_ready"), sem("ysq_ready"), sem("ysum_own")
        grms_ready, grstd_ready, yn_ready = sem("grms_ready"), sem("grstd_ready"), sem("yn_ready")
        mix_hi, mix_lo = sem("mix_hi"), sem("mix_lo")
        tok_ready, tok_read = sem("tok_ready"), sem("tok_read")
        half_done, half_ready, half_sq, half_tok = (
            sem("half_done"), sem("half_ready"), sem("half_sq"), sem("half_tok"))
        tstat, tstd, trstd = sem("tstat"), sem("tstd"), sem("trstd")
        out_even, out_odd = sem("out_even"), sem("out_odd")
        dve_own = sem("dve_own")

        wg = [w[0].rearrange("(k p) f -> p k f", p=P) for w in (t["ffn1_w_gate"], t["ffn2_w_gate"])]
        wu = [w[0].rearrange("(k p) f -> p k f", p=P) for w in (t["ffn1_w_up"], t["ffn2_w_up"])]
        wd = [w[0].rearrange("(k p) f -> p k f", p=P) for w in (t["ffn1_w_down"], t["ffn2_w_down"])]
        w_in = t["w_in"][0].rearrange("(k p) f -> p k f", p=P)
        w_out = t["w_out"][0].rearrange("(k p) f -> p k f", p=P)
        pool_w = t["pool_w"][0].rearrange("g (k p) f -> p (g k) f", p=P)
        Z0, C0, T0, V0 = 0, D, D + CONV, D + CONV + HEADS

        def slot(m):
            return m % RING

        def use(m, i):
            return (m // RING) * 16 + 16 + i * 16

        def half(h):
            return slice(h * HALF, (h + 1) * HALF)

        def doublings(i):
            return U_ORDER[i] // 2 + 1

        def pool_output(engine, q):
            if q % 4 == 3:
                engine.wait_ge(unit_done, M_MIX + U_POOL + q // 4 + 1)
            else:
                engine.wait_ge(pool_mm, q + 1 - (q + 1) // 4)

        blk = ctx.enter_context(nc.Block())

        @blk.sync
        def _(sp):
            def fetch(m, i, src, blocks=UB, width=P):
                if not (isinstance(i, int) and m + RING * i < RING):
                    sp.wait_ge(w_hi, i * RING + (m - RING + 1))
                    sp.wait_ge(w_lo, i * RING + (m - RING + 1))
                dst = raw[:, slot(m), 0:blocks, :]
                if width != P:
                    dst = raw[:, slot(m), :, :].rearrange("p (g c) n -> p g (c n)", c=width // P)
                sp.dma_start(dst, src).then_inc(landed[slot(m)], 16)

            def ffn_fetch(f, m0):
                def gate_up(i):
                    for j in range(4):
                        w = (wg, wu)[j % 2][f]
                        c = i * (2 * P) + (j // 2) * P
                        c = slice(c, c + P) if isinstance(c, int) else bass.ds(c, P)
                        fetch(m0 + j, i, w[:, :, c])
                gate_up(0)
                with sp.Fori(1, FT // 2) as i:
                    gate_up(i)
                with sp.Fori(0, DK) as i:
                    for j in range(4):
                        fetch(m0 + N_GU + j, i, wd[f][:, DOWN0[j]:DOWN0[j] + DOWN[j], block(i)], DOWN[j])

            rows = ((t["ffn1_norm"], R_N1), (t["mix_norm"], R_MIX), (t["ffn2_norm"], R_N2),
                    (t["ssd_norm"], R_SSDN), (t["pool_scale"], R_PS), (t["conv_b"], R_CB))
            for a, r in rows:
                v = a[0].rearrange("(k p) -> k p", p=P)
                sp.dma_start(prow[r:r + v.shape[0], :], v).then_inc(par_landed, 16)
            sp.dma_start(prow[R_CW:R_CW + TAPS * CT, :],
                         t["conv_w"][0].rearrange("w (k p) -> (w k) p", p=P)).then_inc(par_landed, 16)
            sp.wait_ge(x_landed[NC - 2], 16)
            ffn_fetch(0, M_FFN1)
            m = M_MIX
            fetch(m + U_DT, 0, w_in[:, :, T0:T0 + P])
            for i, tile in enumerate(CONV_ORDER):
                fetch(m + U_CONV + i, 0, w_in[:, :, C0 + tile * P:C0 + (tile + 1) * P])
            for i in range(DK):
                fetch(m + U_Z + i, 0, w_in[:, :, Z0 + i * P:Z0 + (i + 1) * P])
            for i, tile in enumerate(U_ORDER):
                fetch(m + U_U + i, 0, w_in[:, :, V0 + tile * P:V0 + (tile + 1) * P])
            for i in range(2):
                fetch(m + U_POOL + i, 0, pool_w[:, 4 - 4 * i:8 - 4 * i, :], width=PG)
            for i in range(DK):
                fetch(m + U_OUTP + i, 0, w_out[:, DK:2 * DK, block(i)])
            for i in range(DK):
                fetch(m + U_OUTS + i, 0, w_out[:, 0:DK, block(i)])
            ffn_fetch(1, M_FFN2)
            for c in range(NC):
                sp.wait_ge((out_even, out_odd)[c % 2], c // 2 + 1)
                sp.dma_start(out[0, block(c), :], xtok[:, c, :]).then_inc(out_landed, 16)
            sp.wait_ge(out_landed, 16 * NC)

        @blk.gpsimd
        def _(pool):
            pool.memset(ident[:, :], 0.0).then_inc(pool_own, 1)
            pool.memset(causal[:, :], 1.0).then_inc(pool_own, 1)
            pool.memset(ones[:, :], 1.0).then_inc(consts, 1)
            pool.memset(eps[:, :], EPS).then_inc(consts, 1)
            pool.wait_ge(pool_own, 2)
            pool.affine_select(out=ident[:, :], in_=ident[:, :], compare_op=ALU.not_equal, fill=1.0,
                               base=0, pattern=[[-1, P]], channel_multiplier=1).then_inc(consts, 1)
            pool.affine_select(out=causal[:, :], in_=causal[:, :], compare_op=ALU.is_ge, fill=0.0,
                               base=0, pattern=[[1, P]], channel_multiplier=-1).then_inc(consts, 1)
            for i in range(PAD):
                pool.memset(inv_count[:, i:i + 1], 1.0 / (i + 1)).then_inc(consts, 1)

            def sum_squares(p, adds=DK):
                if p:
                    pool.wait_ge(rstd_ready, p)
                pool.memset(sumsq[:, :], 0.0).then_inc(sum_own, 1)

                def add(d, e):
                    pool.wait_ge(sq_ready, d + (DK * p + 1))
                    pool.wait_ge(sum_own, d + ((DK + 1) * p + 1))
                    pool.tensor_tensor(sumsq[:, :], sumsq[:, :], sq[:, e, :], ALU.add).then_inc(sum_own, 1)

                with pool.Fori(0, adds // 2) as i:
                    for e in range(2):
                        add(i * 2 + e, e)
                if adds % 2:
                    add(adds - 1, 0)

            def gates(f):
                with pool.Fori(0, FT // 2) as i:
                    for e in range(2):
                        pool.wait_ge(g_silu, i * 2 + (FT * f + e + 1))
                        pool.wait_ge(rstd_ready, 1 + 2 * f)
                        pool.tensor_tensor(gsilu[:, e, :], gsilu[:, e, :], rstd[:, :], ALU.mult).then_inc(g_r, 1)

            sum_squares(0)
            gates(0)
            sum_squares(1)

            pool.wait_ge(unit_done, M_MIX)
            pool.memset(proj[:, :, :], 0.0).then_inc(pads, 1)
            pool.memset(conv[:, :, :], 0.0).then_inc(pads, 1)
            pool.memset(sel32[:, :, :], 0.0).then_inc(pool_own, 1)
            pool.wait_ge(pool_own, 3)
            pool.affine_select(out=sel32[:, :, :], in_=sel32[:, :, :], compare_op=ALU.not_equal, fill=1.0,
                               base=0, pattern=[[1, HEADS], [0, P]], channel_multiplier=-1).then_inc(pool_own, 1)
            pool.wait_ge(pool_own, 4)
            pool.affine_select(out=sel32[:, :, :], in_=sel32[:, :, :], compare_op=ALU.not_equal, fill=1.0,
                               base=LOW, pattern=[[1, HEADS], [0, P]], channel_multiplier=-1).then_inc(sel_made, 1)
            pool.memset(a2[:, :, :], 0.0).then_inc(pads, 1)

            def state_input(j):
                pool.wait_ge(scr_read, SC[f"x{j}"] + 1)
                pool.wait_ge(decay_ready, 1)
                if j >= DK // 2:
                    pool.wait_ge(scr_ready, SC["state02"] + 1)
                w = sm3("wst")[:, 0:NC - 1, 2 * j:2 * j + 2].unsqueeze(3).to_broadcast([P, NC - 1, 2, HD])
                pool.tensor_tensor(
                    xst[:, j % 4, :, :].rearrange("p c (e q) -> p c e q", e=2),
                    xdt[:, j, 0:NC - 1, :].rearrange("p c (e q) -> p c e q", e=2), w, ALU.mult).then_inc(xst_ready, 1)

            def clamp(h):
                pool.wait_ge(d_ready, h + 1)
                pool.tensor_scalar(ebuf[:, h % 2, :], ebuf[:, h % 2, :], 0.0, None, ALU.min).then_inc(min_ready, 1)

            for i in range(CT):
                m = U_CONV + i
                if m == 11:
                    state_input(3)
                if m == 12:
                    clamp(0)
                pool.wait_ge(tap_ready, i + 1)
                pool.wait_ge(conv_done, i + 1)
                pool.tensor_tensor(conv[:, i % 2, PAD:], conv[:, i % 2, PAD:], ebuf[:, i % 2, :],
                                   ALU.add).then_inc(conv_sum, 1)
                if 8 <= m <= 10:
                    state_input(m - 8)
            sums = 4
            for h in range(HEADS):
                if h < 4:
                    state_input(4 + h)
                if h + 1 < HEADS:
                    clamp(h + 1)
                if h >= DK:
                    i = h - DK
                    pool.wait_ge(proj_read, U_U + i + 1)
                    if i:
                        pool.wait_ge(pooled_ready, i)
                    src, shift = proj[:, i % 2, :], 1
                    for step in range(doublings(i)):
                        add = pool.tensor_tensor(conv[:, step % 2, PAD:], src[:, PAD:],
                                                 src[:, PAD - shift:PAD + S - shift], ALU.add)
                        if step < doublings(i) - 1:
                            sums += 1
                            add.then_inc(pool_own, 1)
                            pool.wait_ge(pool_own, sums)
                        else:
                            add.then_inc(win_ready, 1)
                        src, shift = conv[:, step % 2, :], 2 * shift
            pool.wait_ge(y_done, HEADS)
            for g in range(GROUPS):
                pool.memset(cbuf[:, g, :], 0.0).then_inc(ysum_own, 1)
            for j in range(DK):
                pool.wait_ge(ysq_ready, j + 1)
                pool.wait_ge(ysum_own, 2 + j)
                pool.tensor_tensor(cbuf[:, j // 4, :], cbuf[:, j // 4, :], ebuf[:, j % 2, :], ALU.add).then_inc(ysum_own, 1)
            for j in range(DK):
                pool.wait_ge(grstd_ready, j // 4 + 1)
                pool.tensor_tensor(xsT[:, cols(j)], xsT[:, cols(j)], cbuf[:, j // 4, :], ALU.mult).then_inc(yn_ready, 1)
            sum_squares(2)
            gates(1)
            sum_squares(3, DK - 1)

        @blk.scalar
        def _(act):
            def convert(m, i=0):
                act.wait_ge(landed[slot(m)], use(m, i))
                if not (isinstance(i, int) and m + RING * i < RING):
                    act.wait_ge(unit_done, i * RING + (m - RING + 1))
                act.activation(whi[:, slot(m)], raw[:, slot(m)], ACT.Copy).then_inc(w_hi, 1)

            def norm_hi(p, d, gain):
                act.wait_ge(x_ready, d + (DK * p + 1))
                act.activation(xghi[:, cols(d)], xT[:, cols(d)], ACT.Copy,
                               scale=par[:, one(d + gain)]).then_inc(xg_hi, 1)

            def square(p, d, e, x):
                if p:
                    act.wait_ge(rstd_ready, p)
                act.wait_ge(x_ready, d + (DK * p + 1))
                if not (isinstance(d, int) and p == 0 and d < 2):
                    act.wait_ge(sum_own, d + (DK + 1) * p)
                act.activation(sq[:, e, :], x, ACT.Square).then_inc(sq_ready, 1)

            def rms(p):
                act.wait_ge(stat_ready, p + 1)
                act.activation(sq[:, 0, :], PB[6][:, :], ACT.Sqrt, bias=eps[:, 0:1], scale=1.0 / D).then_inc(std_ready, 1)

            def gate_up(f, m0, i, split=0):
                for j in range(4):
                    e, hidden = j // 2, i * 2 + (FT * f + j // 2)
                    if j % 2 == 0:
                        act.wait_ge(g_scaled, hidden + 1)
                        act.activation(gsilu[:, e, :], gscaled[:, e, :], ACT.Silu).then_inc(g_silu, 1)
                    else:
                        act.wait_ge(act_ready, hidden + 1)
                        act.activation(acthi[:, cols(i * 2 + e)], act32[:, e, :], ACT.Copy).then_inc(act_hi, 1)
                    if j >= split:
                        convert(m0 + j + RING, i)

            for c in range(NC):
                act.dma_start(xload[:, c, :], t["x"][0, block(c), :]).then_inc(x_landed[c], 16)
            act.dma_start(dt_bias[:, :], t["dt_bias"][0].rearrange("(h a) -> h a", a=1)).then_inc(alog_landed, 16)
            act.dma_start(a_exp[:, :], t["a_log"][0].partition_broadcast(P)).then_inc(alog_landed, 16)
            act.dma_start(skip_row[:, :], t["d_skip"][0].partition_broadcast(P)).then_inc(alog_landed, 16)
            act.wait_ge(par_T, 1)
            act.activation(par[:, :], PB[0][:, 0:R_ALL], ACT.Copy).then_inc(par_ready, 1)
            act.wait_ge(consts, 4)
            act.wait_ge(par_ready, 1)
            for d in range(DK):
                norm_hi(0, d, R_N1)
                if d == 0:
                    convert(0)
            convert(1)
            for d in range(DK):
                square(0, d, d % 2, xT[:, cols(d)])
                if d in (1, 3):
                    convert(2 + d // 2)
                if d == 5:
                    convert(RING)
            convert(RING + 1)
            rms(0)
            gate_up(0, M_FFN1, 0, split=2)
            with act.Fori(1, FT // 2) as i:
                gate_up(0, M_FFN1, i)
            with act.Fori(0, DK // 2) as i:
                for e in range(2):
                    for j in range(4):
                        if j == 3:
                            square(1, i * 2 + e, e, xT[:, cols(i * 2 + e)])
                            norm_hi(1, i * 2 + e, R_MIX)
                        convert(N_GU + 4 * e + j + RING, i * 2)

            M = M_MIX
            rms(1)
            convert(M + U_DT + RING)
            def silu(i):
                tile = CONV_ORDER[i]
                dst = (xsT[:, cols(tile)] if tile < DK else
                       bT[:, tile - DK, :] if tile < DK + GROUPS else cT[:, tile - DK - GROUPS, :])
                act.wait_ge(conv_sum, i + 1)
                act.activation(dst, conv[:, i % 2, PAD:], ACT.Silu).then_inc(silu_done, 1)

            def exps(h):
                act.wait_ge(d_ready, h + 1)
                act.activation(cbuf[:, h % 2, CH:], PB[4 + h % 2][:, CH:], ACT.Exp).then_inc(ea_ready, 1)
                act.wait_ge(min_ready, h + 1)
                act.activation(ebuf[:, h % 2, :], ebuf[:, h % 2, :], ACT.Exp).then_inc(e_ready, 1)

            for i, tile in enumerate(CONV_ORDER):
                m = U_CONV + i
                convert(M + m + RING)
                if i >= 2:
                    act.wait_ge(silu_done, i - 1)
                act.wait_ge(proj_read, m + 1)
                act.activation(conv[:, i % 2, PAD:], proj[:, i % 2, PAD:], ACT.Identity,
                               bias=par[:, R_CB + tile:R_CB + tile + 1],
                               scale=par[:, R_CW + 3 * CT + tile:R_CW + 3 * CT + tile + 1]).then_inc(conv_id, 1)
                act.activation(ebuf[:, i % 2, :], proj[:, i % 2, PAD - 3:PAD + S - 3], ACT.Copy,
                               scale=par[:, R_CW + tile:R_CW + tile + 1]).then_inc(tap_ready, 1)
                if i:
                    silu(i - 1)
                if m == 3:
                    act.wait_ge(alog_landed, 48)
                    act.activation(a_exp[:, :], a_exp[:, :], ACT.Exp).then_inc(aexp_ready, 1)
                    act.wait_ge(abs_ready, 1)
                    act.activation(sm("e"), sm("absv"), ACT.Exp, scale=-1.0).then_inc(exp_ready, 1)
                if m == 5:
                    act.wait_ge(sel_made, 1)
                    act.activation(sel[:, :, :], sel32[:, :, :], ACT.Copy).then_inc(sel_ready, 1)
                if m == 6:
                    act.wait_ge(scr_read, SC["acs"] + 1)
                    act.activation(acs_split[:, :], acsT[:, :], ACT.Copy).then_inc(acs_hi, 1)
                if m == 8:
                    act.wait_ge(decay_in, 1)
                    act.activation(sm("wst"), sm("wst"), ACT.Exp).then_inc(decay_ready, 1)
                    act.activation(sm("tot"), sm("tot"), ACT.Exp).then_inc(decay_ready, 1)
            exps(0)
            silu(CT - 1)

            def split_hi(i):
                if i == 3:
                    pool_output(act, 1)
                elif i == 2:
                    act.wait_ge(a_bc, HEADS)
                else:
                    act.wait_ge(y_done, DK)
                for k in range(2):
                    act.wait_ge(pooled_ready, 2 * i + k + 1)
                    act.activation(splits[i][0][k][:, :], pooled[:, cols(U_ORDER[2 * i + k])], ACT.Copy).then_inc(sp_hi, 1)

            for h in range(HEADS):
                convert(M + U_Z + h + RING)
                if h + 1 < HEADS:
                    exps(h + 1)
                if h in SPLIT_AT:
                    split_hi(SPLIT_AT.index(h))
            for g in range(4):
                for d in range(2):
                    q, tile = 2 * g + d, U_ORDER[2 * g + d]
                    pool_output(act, q)
                    act.activation(xghi[:, cols(tile)], PB[POOL_BANKS[q]][:, :], ACT.Copy,
                                   scale=par[:, R_PS + tile:R_PS + tile + 1]).then_inc(pool_hi, 1)
                if g == 0:
                    split_hi(3)
                if g % 2:
                    convert(M + U_POOL + g // 2 + RING)
            for j in range(DK):
                act.activation(zT[:, cols(j)], zT[:, cols(j)], ACT.Silu).then_inc(sz_ready, 1)
            for j in range(DK):
                act.wait_ge(yg_ready, j + 1)
                if j >= 2:
                    act.wait_ge(ysum_own, 1 + j)
                act.activation(ebuf[:, j % 2, :], xsT[:, cols(j)], ACT.Square).then_inc(ysq_ready, 1)
                if j % 4 == 3:
                    convert(M + U_OUTP + j // 4 + RING)
            convert(M + U_OUTP + 2 + RING)
            convert(M + U_OUTP + 3 + RING)
            for g in range(GROUPS):
                n = SC[f"stat{g}"]
                act.wait_ge(scr_ready, n + 1)
                act.activation(cbuf[:, g, :], PB[2 + n % 2][:, :], ACT.Sqrt,
                               bias=eps[:, 0:1], scale=1.0 / (HG * HD)).then_inc(grms_ready, 1)
            for i in range(4):
                for j in (2 * i, 2 * i + 1):
                    act.wait_ge(yn_ready, j + 1)
                    act.activation(mixhi[:, cols(j)], xsT[:, cols(j)], ACT.Copy,
                                   scale=par[:, R_SSDN + j:R_SSDN + j + 1]).then_inc(mix_hi, 1)
                convert(M + U_OUTP + 4 + i + RING)
            with act.Fori(0, 2) as i:
                for j in range(4):
                    square(2, i * 4 + j, j % 2, xT[:, cols(i * 4 + j)])
                    norm_hi(2, i * 4 + j, R_N2)
                    convert(M + U_OUTS + j + RING, i)
            rms(2)
            gate_up(1, M_FFN2, 0)
            with act.Fori(1, FT // 2) as i:
                gate_up(1, M_FFN2, i)
            act.wait_ge(g_silu, 2 * FT)
            act.dma_start(gain_out, t["final_norm"].partition_broadcast(P)).then_inc(gain_landed, 16)

            def down(i, last=False):
                for e in range(1 if last else 2):
                    for j in range(4):
                        convert(M_FFN2 + N_GU + 4 * e + j + RING, i * 2)
                        if j == 3:
                            square(3, i * 2 + e, e, xnew[:, e, :])

            with act.Fori(0, DK // 2 - 1) as i:
                down(i)
            down(DK // 2 - 1, last=True)
            act.wait_ge(sum_own, (DK + 1) * 3 + DK - 1)
            for h in range(2):
                act.wait_ge(half_ready, h + 1)
                act.activation(sq[:, 1, half(h)], xnew[:, 1, half(h)], ACT.Square).then_inc(half_sq, 1)
                two = slice(2 * h, 2 * h + 2)
                act.wait_ge(tstat, h + 1)
                act.activation(tok_rms[:, 0, two], PB[LAST_STAT[h]][:, 0:2], ACT.Sqrt,
                               bias=eps[:, 0:1], scale=1.0 / D).then_inc(tstd, 1)
                act.wait_ge(trstd, h + 1)
                act.wait_ge(tok_read, DK + h)
                c = 2 * h + 1
                act.activation(xtok[:, c, :], xtok[:, c, :], ACT.Copy, scale=tok_rms[:, 1, c:c + 1]).then_inc(out_odd, 1)

        @blk.vector
        def _(dve):
            chain = [0]

            def link(ins):
                chain[0] += 1
                ins.then_inc(dve_own, 1)
                dve.wait_ge(dve_own, chain[0])

            def convert(m, i=0):
                dve.wait_ge(w_hi, i * RING + (m + 1))
                dve.tensor_tensor(wlo[:, slot(m)], raw[:, slot(m)], whi[:, slot(m)].bitcast(F32),
                                  ALU.subtract).then_inc(w_lo, 1)

            def norm_lo(p, d, gain):
                dve.wait_ge(xg_hi, d + (DK * p + 1))
                dve.scalar_tensor_tensor(out=xglo[:, cols(d)], in0=xT[:, cols(d)], scalar=par[:, one(d + gain)],
                                         in1=xghi[:, cols(d)].bitcast(F32), op0=ALU.mult,
                                         op1=ALU.subtract).then_inc(xg_lo, 1)

            def inverse(p):
                dve.wait_ge(std_ready, p + 1)
                dve.reciprocal(rstd[:, :], sq[:, 0, :]).then_inc(rstd_ready, 1)
                dve.wait_ge(rstd_ready, p + 1)

            def gate_up(f, m0, i, split=0):
                for j in range(4):
                    e, hidden = j // 2, i * 2 + (FT * f + j // 2)
                    dve.wait_ge(unit_done, i * RING + (m0 + j + 1))
                    if j % 2 == 0:
                        dve.tensor_tensor(gscaled[:, e, :], PB[j][:, :], rstd[:, :], ALU.mult).then_inc(g_scaled, 1)
                    else:
                        dve.wait_ge(g_r, hidden + 1)
                        dve.tensor_tensor(act32[:, e, :], PB[j][:, :], gsilu[:, e, :], ALU.mult).then_inc(act_ready, 1)
                        dve.wait_ge(act_hi, hidden + 1)
                        dve.tensor_tensor(actlo[:, cols(i * 2 + e)], act32[:, e, :],
                                          acthi[:, cols(i * 2 + e)].bitcast(F32), ALU.subtract).then_inc(act_lo, 1)
                    if j >= split:
                        convert(m0 + j + RING, i)

            halves = xT[:, :].rearrange("p (b e h s) -> p b h e s", e=2, h=2, s=S // 2)
            for h in range(2):
                for b in range(4):
                    dve.wait_ge(x_in, (2 * h + 1) * DK + 2 * b + 2)
                    move = dve.tensor_copy(halves[:, b, h, :, :], PB[4 * h + b][:, :].rearrange("p (e s) -> p e s", e=2))
                    move.then_inc(*((x_ready, 2) if h else (x_moved, 1)))
            for d in range(DK):
                norm_lo(0, d, R_N1)
                if d == 0:
                    convert(0)
            for m in range(1, RING + 2):
                convert(m)
            inverse(0)
            gate_up(0, M_FFN1, 0, split=2)
            with dve.Fori(1, FT // 2) as i:
                gate_up(0, M_FFN1, i)

            with dve.Fori(0, DK // 2) as i:
                for e in range(2):
                    for j in range(4):
                        d = i * 2 + e
                        if j == 3:
                            dve.wait_ge(unit_done, i * 8 + (N_GU + 4 * e + 4))
                            dve.scalar_tensor_tensor(out=xT[:, cols(d)], in0=PB[4 + e][:, :], scalar=0.5,
                                                     in1=xT[:, cols(d)], op0=ALU.mult, op1=ALU.add).then_inc(x_ready, 1)
                            norm_lo(1, d, R_MIX)
                        convert(N_GU + 4 * e + j + RING, i * 2)

            M = M_MIX

            def scratch(n):
                dve.wait_ge(scr_ready, n + 1)
                return PB[2 + n % 2]

            def project(q, dst):
                dve.wait_ge(unit_done, M + q + 1)
                rows = dst.shape[0]
                dve.tensor_tensor(dst, PB[q % 2][0:rows, :], rstd[0:rows, :], ALU.mult).then_inc(proj_read, 1)

            def log1p_atanh():
                dve.wait_ge(exp_ready, 1)
                link(dve.tensor_scalar(sm("den"), sm("e"), 2.0, None, ALU.add))
                link(dve.reciprocal(sm("den"), sm("den")))
                link(dve.tensor_tensor(sm("t"), sm("e"), sm("den"), ALU.mult))
                link(dve.tensor_tensor(sm("t2"), sm("t"), sm("t"), ALU.mult))
                link(dve.tensor_scalar(sm("q"), sm("t2"), 1.0 / 17, None, ALU.mult))
                for odd in (15, 13, 11, 9, 7, 5, 3):
                    link(dve.scalar_tensor_tensor(out=sm("q"), in0=sm("q"), scalar=1.0 / odd, in1=sm("t2"),
                                                  op0=ALU.add, op1=ALU.mult))
                link(dve.scalar_tensor_tensor(out=sm("q"), in0=sm("q"), scalar=1.0, in1=sm("t"),
                                              op0=ALU.add, op1=ALU.mult))
                link(dve.tensor_scalar(sm("v"), sm("v"), 0.0, None, ALU.max))
                link(dve.scalar_tensor_tensor(out=sm("dt"), in0=sm("q"), scalar=2.0, in1=sm("v"),
                                              op0=ALU.mult, op1=ALU.add))
                dve.wait_ge(aexp_ready, 1)
                dve.wait_ge(pads, 3)
                for copy in range(2):
                    product = dve.scalar_tensor_tensor(
                        out=a2[:, :, copy * LOW:copy * LOW + HEADS], in0=sm3("dt"), scalar=-1.0,
                        in1=a_exp[:, :].unsqueeze(1).to_broadcast([P, NC, HEADS]), op0=ALU.mult, op1=ALU.mult)
                product.then_inc(a_ready, 1)

            def x_times_dt(j):
                w = sm3("dt")[:, :, 2 * j:2 * j + 2].unsqueeze(3).to_broadcast([P, NC, 2, HD])
                dve.tensor_tensor(xdt[:, j, :, :].rearrange("p c (e q) -> p c e q", e=2),
                                  scratch(SC[f"x{j}"])[:, :].rearrange("p (c e q) -> p c e q", c=NC, e=2),
                                  w, ALU.mult).then_inc(scr_read, 1)

            def state(g, c):
                n = SC[f"state{g}{c}"]
                bank = scratch(n)
                if c == 0:
                    dve.tensor_copy(prev[:, g, 0, :], bank[:, :]).then_inc(scr_read, 1)
                else:
                    if c == 1:
                        dve.wait_ge(decay_ready, 2)
                    dec = sm3("tot")[:, c, HG * g:HG * (g + 1)].unsqueeze(2).to_broadcast([P, HG, HD])
                    view = lambda k: prev[:, g, k, :].rearrange("p (h q) -> p h q", h=HG)
                    link(dve.tensor_tensor(view(c), view(c - 1), dec, ALU.mult))
                    dve.tensor_tensor(prev[:, g, c, :], prev[:, g, c, :], bank[:, :], ALU.add).then_inc(scr_read, 1)
                dve.wait_ge(scr_read, n + 1)

            def difference(h):
                dve.wait_ge(a_bc, h + 1)
                if h >= 2:
                    dve.wait_ge(y_done, h - 1)
                dve.tensor_tensor(ebuf[:, h % 2, :].rearrange("p (c l) -> p c l", c=NC),
                                  PB[4 + h % 2][:, :].rearrange("p (c l) -> p c l", c=NC),
                                  sm3("acs")[:, :, h:h + 1].to_broadcast([P, NC, CH]), ALU.subtract).then_inc(d_ready, 1)

            def weigh(h):
                g = h // HG
                dve.wait_ge(e_ready, h + 1)
                dve.tensor_tensor(ebuf[:, h % 2, :], ebuf[:, h % 2, :], gm[:, g, :], ALU.mult).then_inc(m_ready, 1)
                dve.wait_ge(ea_ready, h + 1)
                dve.tensor_tensor(cbuf[:, h % 2, CH:], cbuf[:, h % 2, CH:], cT[:, g, CH:], ALU.mult).then_inc(ce_ready, 1)

            def skip(p):
                dve.wait_ge(y_done, 2 * p + 2)
                dve.scalar_tensor_tensor(out=xsT[:, cols(p)], in0=xsT[:, cols(p)],
                                         scalar=skip_col[:, p:p + 1], in1=PB[6 + p % 2][:, :],
                                         op0=ALU.mult, op1=ALU.add).then_inc(y_read, 1)

            def pool_mean(i):
                tile = U_ORDER[i]
                n = WINDOWS[tile // 2] - 1
                total = conv[:, (doublings(i) - 1) % 2, :]
                frame = proj[:, i % 2, :]
                dve.wait_ge(win_ready, i + 1)
                dve.scalar_tensor_tensor(out=pooled[:, tile * S + n:(tile + 1) * S], in0=total[:, PAD + n:],
                                         scalar=1.0 / (n + 1), in1=frame[:, PAD + n:], op0=ALU.mult, op1=ALU.subtract)
                head = pooled[:, tile * S:tile * S + n]
                link(dve.tensor_tensor(head, total[:, PAD:PAD + n], inv_count[:, 0:n], ALU.mult))
                dve.tensor_tensor(head, head, frame[:, PAD:PAD + n], ALU.subtract).then_inc(pooled_ready, 1)

            def split_lo(i):
                for k in range(2):
                    dve.wait_ge(sp_hi, 2 * i + k + 1)
                    dve.tensor_tensor(splits[i][1][k][:, :], pooled[:, cols(U_ORDER[2 * i + k])],
                                      splits[i][0][k][:, :].bitcast(F32), ALU.subtract).then_inc(sp_lo, 1)

            inverse(1)
            project(U_DT, dtfm[:, :])
            convert(M + U_DT + RING)
            dve.wait_ge(proj_read, 1)
            dve.wait_ge(alog_landed, 48)
            dve.tensor_scalar(dtfm[:, :], dtfm[:, :], dt_bias[:, 0:1], None, ALU.add).then_inc(dt_fm_ready, 1)
            pairs = skip_row[:, :].rearrange("p (j e) -> p j e", e=2)
            for e in range(2):
                rows = slice(e * HD, (e + 1) * HD)
                link(dve.tensor_copy(skip_col[rows, :], pairs[rows, :, e]))
            dve.wait_ge(pads, 2)
            dve.wait_ge(consts, 4 + PAD)
            for i, tile in enumerate(CONV_ORDER):
                m = U_CONV + i
                if m == 12:
                    state(0, 0)
                    state(0, 1)
                if i >= 2:
                    dve.wait_ge(tap_ready, i - 1)
                project(m, proj[:, i % 2, PAD:])
                if m == 12:
                    dve.wait_ge(conv_sum, i)
                    difference(0)
                convert(M + m + RING)
                dve.wait_ge(conv_id, i + 1)
                for tap in range(1, TAPS - 1):
                    back = TAPS - 1 - tap
                    r = R_CW + tap * CT + tile
                    stt = dve.scalar_tensor_tensor(
                        out=conv[:, i % 2, PAD:], in0=proj[:, i % 2, PAD - back:PAD + S - back], scalar=par[:, r:r + 1],
                        in1=conv[:, i % 2, PAD:], op0=ALU.mult, op1=ALU.add)
                    if tap < TAPS - 2:
                        link(stt)
                    else:
                        stt.then_inc(conv_done, 1)
                if m == 2:
                    dve.tensor_copy(sm("v"), scratch(SC["dt"])[:, 0:NC * HEADS]).then_inc(scr_read, 1)
                    dve.wait_ge(scr_read, SC["dt"] + 1)
                    dve.scalar_tensor_tensor(out=sm("absv"), in0=sm("v"), scalar=-1.0, in1=sm("v"),
                                             op0=ALU.mult, op1=ALU.max).then_inc(abs_ready, 1)
                if m in (3, 4):
                    dve.tensor_copy(btok[:, m - 3, :], scratch(SC[f"b{m - 3}"])[:, :]).then_inc(scr_read, 1)
                if m == 3:
                    log1p_atanh()
                if m == 5:
                    dve.tensor_copy(acsT[:, :], scratch(SC["acs"])[0:SPLIT, :]).then_inc(scr_read, 1)
                if m == 7:
                    dve.wait_ge(acs_hi, 1)
                    low = slice(LOW, SPLIT)
                    dve.tensor_tensor(acs_split[low, :], acsT[low, :], acs_split[low, :].bitcast(F32),
                                      ALU.subtract).then_inc(acs_lo, 1)
                if m == 7:
                    bank = scratch(SC["col"])
                    link(dve.tensor_copy(sm("acs"), bank[:, 64:128]))
                    dve.tensor_copy(sm("tot"), bank[:, 0:64]).then_inc(scr_read, 1)
                    dve.wait_ge(scr_read, SC["col"] + 1)
                    link(dve.tensor_tensor(sm("wst"), sm("tot"), sm("acs"), ALU.subtract))
                    dve.tensor_scalar(sm("wst"), sm("wst"), 0.0, None, ALU.min).then_inc(decay_in, 1)
                if 7 <= m <= 10:
                    x_times_dt(m - 7)
                if m == 10:
                    for g in range(GROUPS):
                        dve.wait_ge(g_mm, g + 1)
                        dve.tensor_tensor(gm[:, g, :].rearrange("p (c l) -> p c l", c=NC),
                                          PB[4 + g][:, :].rearrange("p (c l) -> p c l", c=NC),
                                          causal[:, :].unsqueeze(1).to_broadcast([P, NC, CH]), ALU.mult).then_inc(gm_ready, 1)
                if m == 12:
                    state(0, 2)
            for h in range(HEADS):
                m = U_Z + h
                weigh(h)
                if h >= 2 and h % 2 == 0:
                    skip(h // 2 - 1)
                if h < DK:
                    project(m, zT[:, cols(h)])
                else:
                    u = h - DK
                    dve.wait_ge(unit_done, M + m + 1)
                    if u >= 2:
                        dve.wait_ge(pooled_ready, u - 1)
                    dve.tensor_tensor(proj[:, u % 2, PAD:], PB[m % 2][:, :], rstd[:, :], ALU.mult).then_inc(proj_read, 1)
                if h < 4:
                    x_times_dt(4 + h)
                if h == 5:
                    state(1, 0)
                    state(1, 1)
                if h == 6:
                    state(1, 2)
                if h == 0:
                    dve.wait_ge(conv_sum, CT)
                if h + 1 < HEADS:
                    difference(h + 1)
                convert(M + m + RING)
                if h > DK:
                    pool_mean(h - DK - 1)
                if h in SPLIT_AT:
                    split_lo(SPLIT_AT.index(h))
            pool_mean(DK - 1)
            skip(DK - 1)
            split_lo(3)
            for g in range(4):
                for d in range(2):
                    q, tile = 2 * g + d, U_ORDER[2 * g + d]
                    dve.wait_ge(pool_hi, q + 1)
                    dve.scalar_tensor_tensor(out=xglo[:, cols(tile)], in0=PB[POOL_BANKS[q]][:, :],
                                             scalar=par[:, R_PS + tile:R_PS + tile + 1],
                                             in1=xghi[:, cols(tile)].bitcast(F32),
                                             op0=ALU.mult, op1=ALU.subtract).then_inc(pool_lo, 1)
                if g % 2:
                    convert(M + U_POOL + g // 2 + RING)
            for j in range(DK):
                dve.wait_ge(sz_ready, j + 1)
                dve.tensor_tensor(xsT[:, cols(j)], xsT[:, cols(j)], zT[:, cols(j)], ALU.mult).then_inc(yg_ready, 1)
            for d in range(DK):
                dve.wait_ge(unit_done, M + U_OUTP + d + 1)
                dve.tensor_tensor(xT[:, cols(d)], PB[(U_OUTP + d) % 2][:, :], xT[:, cols(d)], ALU.add).then_inc(proj_read, 1)
                if d >= 4:
                    for j in (2 * (d - 4), 2 * (d - 4) + 1):
                        dve.wait_ge(mix_hi, j + 1)
                        dve.scalar_tensor_tensor(out=mixlo[:, cols(j)], in0=xsT[:, cols(j)],
                                                 scalar=par[:, R_SSDN + j:R_SSDN + j + 1],
                                                 in1=mixhi[:, cols(j)].bitcast(F32),
                                                 op0=ALU.mult, op1=ALU.subtract).then_inc(mix_lo, 1)
                convert(M + U_OUTP + d + RING)
                if d == 3:
                    for g in range(GROUPS):
                        dve.wait_ge(grms_ready, g + 1)
                        dve.reciprocal(cbuf[:, g, :], cbuf[:, g, :]).then_inc(grstd_ready, 1)
            with dve.Fori(0, 2) as i:
                for j in range(4):
                    d = i * 4 + j
                    dve.wait_ge(unit_done, d + (M + U_OUTS + 1))
                    dve.tensor_tensor(xT[:, cols(d)], PB[4 + j % 2][:, :], xT[:, cols(d)], ALU.add).then_inc(x_ready, 1)
                    norm_lo(2, d, R_N2)
                    convert(M + U_OUTS + j + RING, i)
            inverse(2)
            gate_up(1, M_FFN2, 0)
            with dve.Fori(1, FT // 2) as i:
                gate_up(1, M_FFN2, i)

            def tokens(d, e):
                dve.wait_ge(tok_ready, d + 1)
                dve.tensor_tensor(xtok[:, :, block(d)], PB[6 + e][:, :].rearrange("p (c f) -> p c f", c=NC),
                                  gain_out[:, block(d)].unsqueeze(1).to_broadcast([P, NC, P]), ALU.mult).then_inc(tok_read, 1)

            def down(i, last=False):
                for e in range(1 if last else 2):
                    d = i * 2 + e
                    for j in range(4):
                        m = N_GU + 4 * e + j
                        if j == 1 and not (isinstance(i, int) and i == 0 and e == 0):
                            tokens(d - 1, 1 - e)
                        if j == 3:
                            dve.wait_ge(unit_done, i * 8 + (M_FFN2 + m + 1))
                            if not (isinstance(i, int) and i == 0):
                                dve.wait_ge(sq_ready, d + (3 * DK - 1))
                            dve.scalar_tensor_tensor(out=xnew[:, e, :], in0=PB[4 + e][:, :], scalar=0.5,
                                                     in1=xT[:, cols(d)], op0=ALU.mult, op1=ALU.add).then_inc(x_ready, 1)
                        convert(M_FFN2 + m + RING, i * 2)

            dve.wait_ge(gain_landed, 16)
            down(0)
            with dve.Fori(1, DK // 2 - 1) as i:
                down(i)
            down(DK // 2 - 1, last=True)
            tokens(DK - 2, 0)
            d = DK - 1
            dve.wait_ge(sq_ready, 4 * DK - 2)
            for h in range(2):
                dve.wait_ge(half_done, h + 1)
                dve.scalar_tensor_tensor(out=xnew[:, 1, half(h)], in0=PB[LAST_BANK[h]][:, 0:HALF], scalar=0.5,
                                         in1=xT[:, d * S + h * HALF:d * S + (h + 1) * HALF],
                                         op0=ALU.mult, op1=ALU.add).then_inc(half_ready, 1)
                two = slice(2 * h, 2 * h + 2)
                dve.wait_ge(half_tok, h + 1)
                dve.tensor_tensor(xtok[:, two, block(d)],
                                  PB[LAST_TOKENS[h]][:, 0:HALF].rearrange("p (c f) -> p c f", c=2),
                                  gain_out[:, block(d)].unsqueeze(1).to_broadcast([P, 2, P]), ALU.mult).then_inc(tok_read, 1)
                dve.wait_ge(tstd, h + 1)
                dve.reciprocal(tok_rms[:, 1, two], tok_rms[:, 0, two]).then_inc(trstd, 1)
                dve.wait_ge(trstd, h + 1)
                dve.wait_ge(tok_read, DK + h)
                c = 2 * h
                dve.tensor_scalar(xtok[:, c, :], xtok[:, c, :], tok_rms[:, 1, c:c + 1], None, ALU.mult).then_inc(out_even, 1)

        @blk.tensor
        def _(pe):
            def products(bank, m, i, blocks, hi, lo, k0, first=True, last=True, ready=None,
                         order=None, midway=None):
                pe.wait_ge(w_hi, i * RING + (m + 1))
                pe.wait_ge(w_lo, i * RING + (m + 1))
                s = slot(m)
                for n, k in enumerate(order or range(blocks)):
                    if midway and n == blocks // 2:
                        midway()
                    if ready:
                        pe.wait_ge(ready[0], ready[1] + n + 1)
                    h, l = hi[:, cols(k0 + k)], lo[:, cols(k0 + k)]
                    pe.matmul(bank, whi[:, s, k, :], h, start=first and n == 0, stop=False)
                    pe.matmul(bank, whi[:, s, k, :], l, start=False, stop=False)
                    mm = pe.matmul(bank, wlo[:, s, k, :], h, start=False, stop=last and n == blocks - 1)
                mm.then_inc(unit_done, 1)

            def stat(p):
                pe.wait_ge(sum_own, (DK + 1) * (p + 1))
                pe.matmul(PB[6][:, :], ones[:, :], sumsq[:, :], start=True, stop=True).then_inc(stat_ready, 1)

            def gate_up(f, m0, i):
                first = isinstance(i, int)
                for j in range(4):
                    if not first:
                        pe.wait_ge((g_scaled, act_ready)[j % 2], i * 2 + (FT * f + j // 2 - 1))
                    if first and m0 + j == 0:
                        continue
                    products(PB[j][:, :], m0 + j, i, UB, xghi, xglo, 0,
                             ready=(xg_lo, DK * 2 * f) if first and j == 0 else None)
                    if first and j == (2, 0)[f]:
                        stat(2 * f)

            def down(f, m0, i, behind=None, tiles=2):
                for e in range(tiles):
                    d = i * 2 + e
                    for j in range(4):
                        if j == 0:
                            if isinstance(i, int) and i == 0:
                                pe.wait_ge(x_ready, DK * (2 * f + 1))
                            else:
                                pe.wait_ge(x_ready, d + (DK * (2 * f + 1) - 1))
                        pe.wait_ge(act_lo, FT * f + DOWN0[j] + DOWN[j])
                        products(PB[4 + e][:, :], m0 + N_GU + 4 * e + j, i * 2, DOWN[j], acthi, actlo, DOWN0[j],
                                 first=j == 0, last=j == 3)
                        if j == 0 and behind and not (isinstance(i, int) and i == 0 and e == 0):
                            behind(d - 1, 1 - e)

            pe.wait_ge(consts, 4)
            for c in range(NC):
                if c == 3:
                    pe.wait_ge(par_landed, 16 * 7)
                    pe.wait_ge(x_moved, 1)
                    pe.transpose(PB[0][:, 0:R_ALL], prow[0:R_ALL, :], ident[0:R_ALL, 0:R_ALL]).then_inc(par_T, 1)
                pe.wait_ge(x_landed[c], 16)
                for d in range(DK):
                    column = (d % 2) * 2 + c % 2
                    pe.transpose(PB[(c // 2) * 4 + d // 2][:, block(column)], xload[:, c, block(d)],
                                 ident[:, :]).then_inc(x_in, 1)
            pe.wait_ge(x_ready, 2)
            pe.wait_ge(w_hi, 1)
            for k in range(DK):
                pe.wait_ge(xg_hi, k + 1)
                pe.matmul(PB[0][:, :], whi[:, 0, k, :], xghi[:, cols(k)], start=k == 0, stop=False)
            pe.wait_ge(w_lo, 1)
            for k in range(DK):
                pe.wait_ge(xg_lo, k + 1)
                pe.matmul(PB[0][:, :], wlo[:, 0, k, :], xghi[:, cols(k)], start=False, stop=False)
                mm = pe.matmul(PB[0][:, :], whi[:, 0, k, :], xglo[:, cols(k)], start=False, stop=k == DK - 1)
            mm.then_inc(unit_done, 1)

            gate_up(0, M_FFN1, 0)
            with pe.Fori(1, FT // 2) as i:
                gate_up(0, M_FFN1, i)
            down(0, M_FFN1, 0)
            with pe.Fori(1, DK // 2) as i:
                down(0, M_FFN1, i)

            M = M_MIX

            def scratch(n):
                if n >= 2:
                    pe.wait_ge(scr_read, n - 1)
                return PB[2 + n % 2]

            def project(m, ready=None, midway=None):
                if m >= 2:
                    pe.wait_ge(proj_read, m - 1)
                products(PB[m % 2][:, :], M + m, 0, UB, xghi, xglo, 0, ready=ready, midway=midway)

            def chunks_to_tokens(bank, src, width=P, off=0, rows=P):
                for c in range(NC):
                    mm = pe.transpose(bank[:, off + c * width:off + (c + 1) * width], src[:, block(c)],
                                      ident[0:rows, 0:rows])
                return mm

            def x_to_tokens(j):
                pe.wait_ge(silu_done, 4 + j + 1)
                chunks_to_tokens(scratch(SC[f"x{j}"]), xsT[:, cols(j)]).then_inc(scr_ready, 1)

            def state_products(g, c):
                pe.wait_ge(xst_ready, 4 * (g + 1))
                pe.matmul(scratch(SC[f"state{g}{c}"])[:, :].rearrange("p (j f) -> p j f", j=4), btok[:, g, block(c)],
                          xst[:, :, c, :], start=True, stop=True).then_inc(scr_ready, 1)

            def decay_rows(h):
                if h < 2:
                    pe.wait_ge(gm_ready, h + 1)
                else:
                    pe.wait_ge(ea_ready, h - 1)
                pe.matmul(PB[4 + h % 2][:, :], sel[:, h, :], acs_split[:, :], start=True, stop=True).then_inc(a_bc, 1)

            def scan(h):
                g, tile, lo = h // HG, h // 2, (h % 2) * HD
                if h % 2 == 0 and tile >= 2:
                    pe.wait_ge(y_read, tile - 1)
                pe.wait_ge(m_ready, h + 1)
                pe.wait_ge(ce_ready, h + 1)
                for c in range(NC):
                    dst = PB[6 + tile % 2][lo:lo + HD, block(c)]
                    mm = pe.matmul(dst, xdt[:, tile, c, lo:lo + HD], ebuf[:, h % 2, block(c)], start=True, stop=c == 0)
                    if c:
                        q = (h % HG) * HD
                        mm = pe.matmul(dst, prev[:, g, c - 1, q:q + HD], cbuf[:, h % 2, block(c)], start=False, stop=True)
                mm.then_inc(y_done, 1)

            def first_states():
                state_products(0, 0)
                state_products(0, 1)

            project(U_DT, ready=(xg_lo, DK))
            stat(1)
            for i in range(CT):
                m = U_CONV + i
                if m == 12:
                    pe.wait_ge(acs_lo, 1)
                    pe.wait_ge(sel_ready, 1)
                    decay_rows(0)
                project(m, midway=first_states if m == 12 else None)
                if m == 2:
                    pe.wait_ge(dt_fm_ready, 1)
                    chunks_to_tokens(scratch(SC["dt"]), dtfm, width=HEADS, rows=HEADS).then_inc(scr_ready, 1)
                if m in (3, 4):
                    pe.wait_ge(silu_done, m - 2)
                    chunks_to_tokens(scratch(SC[f"b{m - 3}"]), bT[:, m - 3, :]).then_inc(scr_ready, 1)
                if m == 5:
                    pe.wait_ge(a_ready, 1)
                    bank = scratch(SC["acs"])
                    for c in range(NC):
                        mm = pe.matmul(bank[0:SPLIT, block(c)], a2[:, c, :], causal[:, :], start=True, stop=True)
                    mm.then_inc(scr_ready, 1)
                if m == 7:
                    pe.wait_ge(scr_read, SC["acs"] + 1)
                    bank = scratch(SC["col"])
                    pe.matmul(bank[:, 0:NC * HEADS].rearrange("p (c h) -> p c h", c=NC), ones[:, :], a2[:, :, 0:HEADS], start=True, stop=True)
                    chunks_to_tokens(bank, acsT[0:HEADS, :], width=HEADS, off=NC * HEADS, rows=HEADS).then_inc(scr_ready, 1)
                if 7 <= m <= 10:
                    x_to_tokens(m - 7)
                if m == 10:
                    for g in range(GROUPS):
                        for c in range(NC):
                            mm = pe.matmul(PB[4 + g][:, block(c)], bT[:, g, block(c)], cT[:, g, block(c)],
                                           start=True, stop=True)
                        mm.then_inc(g_mm, 1)
                if m == 12:
                    state_products(0, 2)
            for h in range(HEADS):
                project(U_Z + h)
                if h < 4:
                    x_to_tokens(4 + h)
                if h == 5:
                    state_products(1, 0)
                    state_products(1, 1)
                if h == 6:
                    state_products(1, 2)
                if h + 1 < HEADS:
                    decay_rows(h + 1)
                scan(h)
            for g in range(4):
                m = M + U_POOL + g // 2
                if g % 2 == 0:
                    pe.wait_ge(w_hi, m + 1)
                    pe.wait_ge(w_lo, m + 1)
                pe.wait_ge(sp_lo, 2 * g + 2)
                hi, lo = splits[g]
                for d in range(2):
                    q = 2 * g + d
                    pe.wait_ge(*((proj_read, U_POOL - 1), (proj_read, U_POOL), (scr_read, SC["state12"]),
                                 (scr_read, SC["state12"] + 1), (ea_ready, HEADS - 1), (ea_ready, HEADS),
                                 (y_read, DK - 1), (y_read, DK))[q])
                    bank = PB[POOL_BANKS[q]][:, :]
                    for k in range(2):
                        b = (1 - g % 2) * 4 + 2 * k + d
                        pe.matmul(bank, whi[:, slot(m), b, :], hi[k][:, :], start=k == 0, stop=False)
                        pe.matmul(bank, whi[:, slot(m), b, :], lo[k][:, :], start=False, stop=False)
                        mm = pe.matmul(bank, wlo[:, slot(m), b, :], hi[k][:, :], start=False, stop=k == 1)
                    mm.then_inc(unit_done if q % 4 == 3 else pool_mm, 1)
            for d in range(DK):
                if d >= 2:
                    pe.wait_ge(proj_read, U_POOL + d - 1)
                products(PB[(U_OUTP + d) % 2][:, :], M + U_OUTP + d, 0, UB, xghi, xglo, 0,
                         ready=(pool_lo, 0) if d == 0 else None, order=U_ORDER if d == 0 else None)
                if d == 3:
                    for g in range(GROUPS):
                        pe.wait_ge(ysum_own, 2 + 4 * (g + 1))
                        pe.matmul(scratch(SC[f"stat{g}"])[:, :], ones[:, :], cbuf[:, g, :],
                                  start=True, stop=True).then_inc(scr_ready, 1)
            with pe.Fori(0, 2) as i:
                for j in range(4):
                    d = i * 4 + j
                    pe.wait_ge(x_ready, d + (2 * DK - 1))
                    products(PB[4 + j % 2][:, :], M + U_OUTS + j, i, UB, mixhi, mixlo, 0,
                             ready=(mix_lo, 0) if j == 0 else None)
            gate_up(1, M_FFN2, 0)
            with pe.Fori(1, FT // 2) as i:
                gate_up(1, M_FFN2, i)

            def to_tokens(d, e):
                pe.wait_ge(x_ready, d + (3 * DK + 1))
                if not (isinstance(d, int) and d < 2):
                    pe.wait_ge(tok_read, d - 1)
                for c in range(NC):
                    mm = pe.transpose(PB[6 + e][:, block(c)], xnew[:, e, block(c)], ident[:, :])
                mm.then_inc(tok_ready, 1)

            down(1, M_FFN2, 0, to_tokens)
            with pe.Fori(1, DK // 2 - 1) as i:
                down(1, M_FFN2, i, to_tokens)
            down(1, M_FFN2, DK // 2 - 1, to_tokens, tiles=1)

            def finish(h):
                pe.wait_ge(half_ready, h + 1)
                for c in range(2):
                    mm = pe.transpose(PB[LAST_TOKENS[h]][:, block(c)], xnew[:, 1, block(2 * h + c)], ident[:, :])
                mm.then_inc(half_tok, 1)
                pe.wait_ge(sum_own, (DK + 1) * 4 - 1)
                pe.wait_ge(half_sq, h + 1)
                for c in range(2):
                    total = PB[LAST_STAT[h]][:, c:c + 1]
                    pe.matmul(total, sumsq[:, block(2 * h + c)], ones[:, 0:1], start=True, stop=False)
                    mm = pe.matmul(total, sq[:, 1, block(2 * h + c)], ones[:, 0:1], start=False, stop=True)
                mm.then_inc(tstat, 1)

            pe.wait_ge(x_ready, 4 * DK - 2)
            pe.wait_ge(tok_read, DK - 2)
            for h in range(2):
                for j in range(4):
                    m = M_FFN2 + N_GU + 4 * (DK - 1) + j
                    pe.wait_ge(w_hi, m + 1)
                    pe.wait_ge(w_lo, m + 1)
                    for k in range(DOWN[j]):
                        t0 = (DOWN0[j] + k) * S + h * HALF
                        hi, lo = acthi[:, t0:t0 + HALF], actlo[:, t0:t0 + HALF]
                        bank = PB[LAST_BANK[h]][:, 0:HALF]
                        first, last = j == 0 and k == 0, j == 3 and k == DOWN[3] - 1
                        pe.matmul(bank, whi[:, slot(m), k, :], hi, start=first, stop=False)
                        pe.matmul(bank, whi[:, slot(m), k, :], lo, start=False, stop=False)
                        mm = pe.matmul(bank, wlo[:, slot(m), k, :], hi, start=False, stop=last)
                    if j == 0:
                        if h:
                            finish(0)
                        else:
                            to_tokens(DK - 2, 0)
                mm.then_inc(half_done, 1)
            finish(1)


_INS = ["x", "ffn1_norm", "ffn1_w_gate", "ffn1_w_up", "ffn1_w_down", "mix_norm", "w_in", "conv_w", "conv_b",
        "dt_bias", "a_log", "d_skip", "ssd_norm", "pool_w", "pool_scale", "w_out", "ffn2_norm",
        "ffn2_w_gate", "ffn2_w_up", "ffn2_w_down", "final_norm"]


def kernel(**inputs):
    import concourse.bacc as bacc
    from concourse.bass_utils import run_bass_kernel_spmd

    nc = bacc.Bacc("TRN2", target_bir_lowering=False, num_devices=1, dynamic_dma_scratch_size=1024)
    arrays, aps = {}, {}
    for name in _INS:
        a = np.ascontiguousarray(inputs[name])
        arrays["in_" + name] = a
        aps[name] = nc.dram_tensor("in_" + name, a.shape, mybir.dt.from_np(a.dtype), kind="ExternalInput").ap()
    out = nc.dram_tensor("out", (1, S, D), F32, kind="ExternalOutput").ap()
    build(nc, aps, out)
    return run_bass_kernel_spmd(nc, [arrays], core_ids=[0]).results[0]["out"]
```

```python
from contextlib import ExitStack

import numpy as np

import concourse.bass as bass
from concourse import mybir

F32 = mybir.dt.float32
F32R = mybir.dt.float32r
ALU = mybir.AluOpType
ACT = mybir.ActivationFunctionType

P = 128
S = 512
D = 1024
DK = D // P
DFF = 2816
FT = DFF // P
EPS = 1e-6

HEADS = 16
HD = D // HEADS
GROUPS = 2
HG = HEADS // GROUPS
LOW = 32
SPLIT = LOW + HEADS
STATE = 128
CH = 128
NC = S // CH
HALF = S // 2
TAPS = 4
CONV = D + 2 * GROUPS * STATE
CT = CONV // P
WINDOWS = (2, 4, 8, 16)
PG = D // len(WINDOWS)
PAD = 16

RING = 4
UB = 8
DOWN = (6, 6, 5, 5)
DOWN0 = (0, 6, 12, 17)

LAST_BANK, LAST_TOKENS, LAST_STAT = (5, 1), (7, 3), (0, 2)

N_GU = 2 * FT
N_DOWN = 4 * DK
M_FFN1 = 0
M_MIX = N_GU + N_DOWN
U_DT = 0
U_CONV = 1
U_Z = U_CONV + CT
U_U = U_Z + DK
U_POOL = U_U + DK
U_OUTP = U_POOL + 2
U_OUTS = U_OUTP + DK
M_FFN2 = M_MIX + U_OUTS + DK

CONV_ORDER = (8, 9, 10, 11, 0, 1, 2, 3, 4, 5, 6, 7)

R_N1, R_MIX, R_N2, R_CW, R_CB = 0, 8, 16, 24, 24 + TAPS * CT
R_SSDN = R_CB + CT
R_PS = R_SSDN + DK
R_ALL = R_PS + DK

POOL_BANKS = (1, 0, 2, 3, 4, 5, 6, 7)

SCRATCH = ("dt", "b0", "b1", "acs", "col", "x0", "x1", "x2", "x3", "state00", "state01", "state02",
           "x4", "x5", "x6", "x7", "state10", "state11", "state12", "stat0", "stat1")
SC = {name: i for i, name in enumerate(SCRATCH)}

U_ORDER = (6, 7, 4, 5, 2, 3, 0, 1)
SPLIT_AT = (12, 14, 15)


def cols(tile):
    return slice(tile * S, (tile + 1) * S) if isinstance(tile, int) else bass.ds(tile * S, S)


def block(tile):
    return slice(tile * P, (tile + 1) * P) if isinstance(tile, int) else bass.ds(tile * P, P)


def one(i):
    return slice(i, i + 1) if isinstance(i, int) else bass.ds(i, 1)


def build(nc, t, out):
    with ExitStack() as ctx:
        def sb(name, shape, dt=F32):
            return ctx.enter_context(nc.sbuf_tensor(name, shape, dt))

        def sem(name):
            return ctx.enter_context(nc.semaphore(name))

        raw = sb("w_raw", [P, RING, UB, P])
        whi = sb("w_hi_part", [P, RING, UB, P], F32R)
        wlo = sb("w_lo_part", [P, RING, UB, P], F32R)
        xT = sb("xT", [P, DK * S])
        xghi = sb("xghi", [P, DK * S], F32R)
        xglo = sb("xglo", [P, DK * S], F32R)
        rstd = sb("rstd", [P, S])
        sq = sb("sq", [P, 2, S])
        sumsq = sb("sumsq", [P, S])
        ones = sb("ones", [P, P])
        ident = sb("ident", [P, P])
        causal = sb("causal", [P, P])
        par = sb("par", [P, R_ALL])
        eps = sb("eps", [P, 1])
        inv_count = sb("inv_count", [P, PAD])
        dt_bias = sb("dt_bias", [HEADS, 1])
        a_exp = sb("a_exp", [P, HEADS])
        skip_row = sb("skip_row", [P, HEADS])
        skip_col = sb("skip_col", [P, DK])
        tok_rms = sb("tok_rms", [P, 2, NC])

        base = (nc.sbuf_base + 63) // 64 * 64

        def at(name, offset, shape, dt=F32):
            return nc.alloc_sbuf_tensor_at(name, shape, dt, offset=base + offset)

        KB = 1024
        acthi = at("acthi", 0, [P, FT * S], F32R)
        actlo = at("actlo", 44 * KB, [P, FT * S], F32R)
        xload = at("xload", 0, [P, NC, D])
        prow = at("prow", 16 * KB, [P, P])
        gate_buf = at("gate_buf", 88 * KB, [P, 2, D])
        gscaled = gate_buf[:, 0, :].rearrange("p (e s) -> p e s", e=2)
        gsilu = gate_buf[:, 1, :].rearrange("p (e s) -> p e s", e=2)
        gain_out = gate_buf[:, 0, :]
        act32 = at("act32", 96 * KB, [P, 2, S])
        xnew = act32
        xtok = at("xtok", 100 * KB, [P, NC, D])

        xdt = at("xdt", 0, [P, DK, NC, P])
        prev = at("prev", 16 * KB, [P, GROUPS, NC - 1, HG * HD])
        gm = at("gm", 28 * KB, [P, GROUPS, S])
        mixhi = at("mixhi", 0, [P, DK * S], F32R)
        mixlo = at("mixlo", 16 * KB, [P, DK * S], F32R)
        sp0 = [[at(f"sp0{n}{k}", (4 * i + 2 * k) * KB, [P, S], F32R) for k in range(2)]
               for i, n in enumerate("hl")]
        sp1 = [[at("sp1h0", 16 * KB, [P, S], F32R), at("sp1h1", 18 * KB, [P, S], F32R)],
               [at("sp1l0", 20 * KB, [P, S], F32R), at("sp1l1", 28 * KB, [P, S], F32R)]]
        xsT = at("xsT", 32 * KB, [P, DK * S])
        zT = at("zT", 48 * KB, [P, DK * S])
        sel32 = at("sel32", 48 * KB, [SPLIT, HEADS, P])
        pooled = at("pooled", 64 * KB, [P, DK * S])
        xst = at("xst", 64 * KB, [P, DK // 2, NC - 1, P])
        bT = at("bT", 70 * KB, [P, GROUPS, S])
        btok = at("btok", 74 * KB, [P, GROUPS, S])
        cT = at("cT", 80 * KB, [P, GROUPS, S])
        proj = at("proj", 84 * KB, [P, 2, PAD + S])
        conv = at("conv", 84 * KB + 4224, [P, 2, PAD + S])
        o = 84 * KB + 8448
        ebuf = at("ebuf", o, [P, 2, S])
        cbuf = at("cbuf", o + 4096, [P, 2, S])
        sel = at("sel", o + 8192, [SPLIT, HEADS, P], F32R)
        sp2 = [[at(f"sp2{n}{k}", o + 8192 + 2048 * (2 * i + k), [P, S], F32R) for k in range(2)]
               for i, n in enumerate("hl")]
        splits = (sp0, sp1, sp2, sp0)
        acs_split = at("acs_split", o + 16384, [SPLIT, S], F32R)
        dtfm = at("dtfm", o + 4096, [HEADS, S])
        acsT = at("acsT", o + 6144, [SPLIT, S])
        small = {}
        for i, name in enumerate(("v", "absv", "e", "den", "t", "t2", "q", "dt", "acs", "tot", "wst")):
            small[name] = at("tok_" + name, o + 18432 + 256 * i, [P, NC * HEADS])
        a2 = at("tok_a", o + 18432 + 256 * len(small), [P, NC, SPLIT])
        sm = lambda name: small[name][:, :]
        sm3 = lambda name: small[name][:, :].rearrange("p (c h) -> p c h", c=NC)
        assert base + o + 18432 + 256 * len(small) + 4 * NC * SPLIT <= nc.sbuf_usable_end

        PB = [ctx.enter_context(nc.psum_tensor(f"bank{i}", [P, S], F32)) for i in range(8)]

        landed = [sem(f"landed{i}") for i in range(RING)]
        w_hi, w_lo = sem("w_hi"), sem("w_lo")
        unit_done = sem("unit_done")
        x_landed = [sem(f"x_landed{i}") for i in range(DK // 2)]
        norm_landed, par_landed, alog_landed, gain_landed = (
            sem("norm_landed"), sem("par_landed"), sem("alog_landed"), sem("gain_landed"))
        out_landed = sem("out_landed")
        consts, pool_own = sem("consts"), sem("pool_own")
        x_in, x_ready = sem("x_in"), sem("x_ready")
        par_T, par_ready = sem("par_T"), sem("par_ready")
        xg_hi, xg_lo = sem("xg_hi"), sem("xg_lo")
        sq_ready, sum_own = sem("sq_ready"), sem("sum_own")
        stat_ready, std_ready, rstd_ready = sem("stat_ready"), sem("std_ready"), sem("rstd_ready")
        g_scaled, g_silu, g_r = sem("g_scaled"), sem("g_silu"), sem("g_r")
        act_ready, act_hi, act_lo = sem("act_ready"), sem("act_hi"), sem("act_lo")
        proj_read = sem("proj_read")
        pads, sel_made, sel_ready = sem("pads"), sem("sel_made"), sem("sel_ready")
        conv_id, tap_ready, conv_done, conv_sum, silu_done = (
            sem("conv_id"), sem("tap_ready"), sem("conv_done"), sem("conv_sum"), sem("silu_done"))
        scr_ready, scr_read = sem("scr_ready"), sem("scr_read")
        dt_fm_ready, abs_ready, exp_ready, aexp_ready = (
            sem("dt_fm_ready"), sem("abs_ready"), sem("exp_ready"), sem("aexp_ready"))
        a_ready, acs_hi, acs_lo = sem("a_ready"), sem("acs_hi"), sem("acs_lo")
        decay_in, decay_ready = sem("decay_in"), sem("decay_ready")
        g_mm, gm_ready = sem("g_mm"), sem("gm_ready")
        xst_ready = sem("xst_ready")
        a_bc, d_ready, e_ready, ea_ready = sem("a_bc"), sem("d_ready"), sem("e_ready"), sem("ea_ready")
        m_ready, ce_ready, y_done, y_read = sem("m_ready"), sem("ce_ready"), sem("y_done"), sem("y_read")
        win_ready, pooled_ready = sem("win_ready"), sem("pooled_ready")
        sp_hi, sp_lo, pool_mm, pool_hi, pool_lo = (
            sem("sp_hi"), sem("sp_lo"), sem("pool_mm"), sem("pool_hi"), sem("pool_lo"))
        sz_ready, yg_ready, ysq_ready, ysum_own = (
            sem("sz_ready"), sem("yg_ready"), sem("ysq_ready"), sem("ysum_own"))
        grms_ready, grstd_ready, yn_ready = sem("grms_ready"), sem("grstd_ready"), sem("yn_ready")
        mix_hi, mix_lo = sem("mix_hi"), sem("mix_lo")
        tok_ready, tok_read = sem("tok_ready"), sem("tok_read")
        half_done, half_ready, half_sq, half_tok = (
            sem("half_done"), sem("half_ready"), sem("half_sq"), sem("half_tok"))
        tstat, tstd, trstd = sem("tstat"), sem("tstd"), sem("trstd")
        out_even, out_odd = sem("out_even"), sem("out_odd")
        dve_own = sem("dve_own")

        wg = [w[0].rearrange("(k p) f -> p k f", p=P) for w in (t["ffn1_w_gate"], t["ffn2_w_gate"])]
        wu = [w[0].rearrange("(k p) f -> p k f", p=P) for w in (t["ffn1_w_up"], t["ffn2_w_up"])]
        wd = [w[0].rearrange("(k p) f -> p k f", p=P) for w in (t["ffn1_w_down"], t["ffn2_w_down"])]
        w_in = t["w_in"][0].rearrange("(k p) f -> p k f", p=P)
        w_out = t["w_out"][0].rearrange("(k p) f -> p k f", p=P)
        pool_w = t["pool_w"][0].rearrange("g (k p) f -> p (g k) f", p=P)
        Z0, C0, T0, V0 = 0, D, D + CONV, D + CONV + HEADS

        def slot(m):
            return m % RING

        def use(m, i):
            return (m // RING) * 16 + 16 + i * 16

        def half(h):
            return slice(h * HALF, (h + 1) * HALF)

        def doublings(i):
            return U_ORDER[i] // 2 + 1

        def pool_output(engine, q):
            if q % 4 == 3:
                engine.wait_ge(unit_done, M_MIX + U_POOL + q // 4 + 1)
            else:
                engine.wait_ge(pool_mm, q + 1 - (q + 1) // 4)

        blk = ctx.enter_context(nc.Block())

        @blk.sync
        def _(sp):
            def fetch(m, i, src, blocks=UB, width=P):
                if isinstance(i, int) and m + RING * i == 1:
                    sp.wait_ge(x_landed[-2], 16)
                if not (isinstance(i, int) and m + RING * i < RING):
                    sp.wait_ge(w_hi, i * RING + (m - RING + 1))
                    sp.wait_ge(w_lo, i * RING + (m - RING + 1))
                dst = raw[:, slot(m), 0:blocks, :]
                if width != P:
                    dst = raw[:, slot(m), :, :].rearrange("p (g c) n -> p g (c n)", c=width // P)
                sp.dma_start(dst, src).then_inc(landed[slot(m)], 16)

            def ffn_fetch(f, m0):
                def gate_up(i):
                    for j in range(4):
                        w = (wg, wu)[j % 2][f]
                        c = i * (2 * P) + (j // 2) * P
                        c = slice(c, c + P) if isinstance(c, int) else bass.ds(c, P)
                        fetch(m0 + j, i, w[:, :, c])
                gate_up(0)
                with sp.Fori(1, FT // 2) as i:
                    gate_up(i)
                with sp.Fori(0, DK) as i:
                    for j in range(4):
                        fetch(m0 + N_GU + j, i, wd[f][:, DOWN0[j]:DOWN0[j] + DOWN[j], block(i)], DOWN[j])

            rows = ((t["ffn1_norm"], R_N1), (t["mix_norm"], R_MIX), (t["ffn2_norm"], R_N2),
                    (t["ssd_norm"], R_SSDN), (t["pool_scale"], R_PS), (t["conv_b"], R_CB))
            for a, r in rows:
                v = a[0].rearrange("(k p) -> k p", p=P)
                sp.dma_start(prow[r:r + v.shape[0], :], v).then_inc(par_landed if r else norm_landed, 16)
            sp.dma_start(prow[R_CW:R_CW + TAPS * CT, :],
                         t["conv_w"][0].rearrange("w (k p) -> (w k) p", p=P)).then_inc(par_landed, 16)
            sp.wait_ge(x_landed[0], 16)
            ffn_fetch(0, M_FFN1)
            sp.dma_start(dt_bias[:, :], t["dt_bias"][0].rearrange("(h a) -> h a", a=1)).then_inc(alog_landed, 16)
            sp.dma_start(a_exp[:, :], t["a_log"][0].partition_broadcast(P)).then_inc(alog_landed, 16)
            sp.dma_start(skip_row[:, :], t["d_skip"][0].partition_broadcast(P)).then_inc(alog_landed, 16)
            m = M_MIX
            fetch(m + U_DT, 0, w_in[:, :, T0:T0 + P])
            for i, tile in enumerate(CONV_ORDER):
                fetch(m + U_CONV + i, 0, w_in[:, :, C0 + tile * P:C0 + (tile + 1) * P])
            for i in range(DK):
                fetch(m + U_Z + i, 0, w_in[:, :, Z0 + i * P:Z0 + (i + 1) * P])
            for i, tile in enumerate(U_ORDER):
                fetch(m + U_U + i, 0, w_in[:, :, V0 + tile * P:V0 + (tile + 1) * P])
            for i in range(2):
                fetch(m + U_POOL + i, 0, pool_w[:, 4 - 4 * i:8 - 4 * i, :], width=PG)
            for i in range(DK):
                fetch(m + U_OUTP + i, 0, w_out[:, DK:2 * DK, block(i)])
            for i in range(DK):
                fetch(m + U_OUTS + i, 0, w_out[:, 0:DK, block(i)])
            ffn_fetch(1, M_FFN2)
            for c in range(NC):
                sp.wait_ge((out_even, out_odd)[c % 2], c // 2 + 1)
                sp.dma_start(out[0, block(c), :], xtok[:, c, :]).then_inc(out_landed, 16)
            sp.wait_ge(out_landed, 16 * NC)

        @blk.gpsimd
        def _(pool):
            pool.memset(ident[:, :], 0.0).then_inc(pool_own, 1)
            pool.memset(causal[:, :], 1.0).then_inc(pool_own, 1)
            pool.memset(ones[:, :], 1.0).then_inc(consts, 1)
            pool.memset(eps[:, :], EPS).then_inc(consts, 1)
            pool.wait_ge(pool_own, 2)
            pool.affine_select(out=ident[:, :], in_=ident[:, :], compare_op=ALU.not_equal, fill=1.0,
                               base=0, pattern=[[-1, P]], channel_multiplier=1).then_inc(consts, 1)
            pool.affine_select(out=causal[:, :], in_=causal[:, :], compare_op=ALU.is_ge, fill=0.0,
                               base=0, pattern=[[1, P]], channel_multiplier=-1).then_inc(consts, 1)
            for i in range(PAD):
                pool.memset(inv_count[:, i:i + 1], 1.0 / (i + 1)).then_inc(consts, 1)

            def sum_squares(p, adds=DK):
                if p:
                    pool.wait_ge(rstd_ready, p)
                pool.memset(sumsq[:, :], 0.0).then_inc(sum_own, 1)

                def add(d, e):
                    pool.wait_ge(sq_ready, d + (DK * p + 1))
                    pool.wait_ge(sum_own, d + ((DK + 1) * p + 1))
                    pool.tensor_tensor(sumsq[:, :], sumsq[:, :], sq[:, e, :], ALU.add).then_inc(sum_own, 1)

                with pool.Fori(0, adds // 2) as i:
                    for e in range(2):
                        add(i * 2 + e, e)
                if adds % 2:
                    add(adds - 1, 0)

            def gates(f):
                with pool.Fori(0, FT // 2) as i:
                    for e in range(2):
                        pool.wait_ge(g_silu, i * 2 + (FT * f + e + 1))
                        pool.wait_ge(rstd_ready, 1 + 2 * f)
                        pool.tensor_tensor(gsilu[:, e, :], gsilu[:, e, :], rstd[:, :], ALU.mult).then_inc(g_r, 1)

            sum_squares(0)
            gates(0)
            sum_squares(1)

            pool.wait_ge(unit_done, M_MIX)
            pool.memset(proj[:, :, :], 0.0).then_inc(pads, 1)
            pool.memset(conv[:, :, :], 0.0).then_inc(pads, 1)
            pool.memset(sel32[:, :, :], 0.0).then_inc(pool_own, 1)
            pool.wait_ge(pool_own, 3)
            pool.affine_select(out=sel32[:, :, :], in_=sel32[:, :, :], compare_op=ALU.not_equal, fill=1.0,
                               base=0, pattern=[[1, HEADS], [0, P]], channel_multiplier=-1).then_inc(pool_own, 1)
            pool.wait_ge(pool_own, 4)
            pool.affine_select(out=sel32[:, :, :], in_=sel32[:, :, :], compare_op=ALU.not_equal, fill=1.0,
                               base=LOW, pattern=[[1, HEADS], [0, P]], channel_multiplier=-1).then_inc(sel_made, 1)
            pool.memset(a2[:, :, :], 0.0).then_inc(pads, 1)

            def state_input(j):
                pool.wait_ge(scr_read, SC[f"x{j}"] + 1)
                pool.wait_ge(decay_ready, 1)
                if j >= DK // 2:
                    pool.wait_ge(scr_ready, SC["state02"] + 1)
                w = sm3("wst")[:, 0:NC - 1, 2 * j:2 * j + 2].unsqueeze(3).to_broadcast([P, NC - 1, 2, HD])
                pool.tensor_tensor(
                    xst[:, j % 4, :, :].rearrange("p c (e q) -> p c e q", e=2),
                    xdt[:, j, 0:NC - 1, :].rearrange("p c (e q) -> p c e q", e=2), w, ALU.mult).then_inc(xst_ready, 1)

            for i in range(CT):
                m = U_CONV + i
                if m == 11:
                    state_input(3)
                pool.wait_ge(tap_ready, i + 1)
                pool.wait_ge(conv_done, i + 1)
                pool.tensor_tensor(conv[:, i % 2, PAD:], conv[:, i % 2, PAD:], ebuf[:, i % 2, :],
                                   ALU.add).then_inc(conv_sum, 1)
                if 8 <= m <= 10:
                    state_input(m - 8)
            sums = 4
            for h in range(HEADS):
                if h < 4:
                    state_input(4 + h)
                if h >= DK:
                    i = h - DK
                    pool.wait_ge(proj_read, U_U + i + 1)
                    if i:
                        pool.wait_ge(pooled_ready, i)
                    src, shift = proj[:, i % 2, :], 1
                    for step in range(doublings(i)):
                        add = pool.tensor_tensor(conv[:, step % 2, PAD:], src[:, PAD:],
                                                 src[:, PAD - shift:PAD + S - shift], ALU.add)
                        if step < doublings(i) - 1:
                            sums += 1
                            add.then_inc(pool_own, 1)
                            pool.wait_ge(pool_own, sums)
                        else:
                            add.then_inc(win_ready, 1)
                        src, shift = conv[:, step % 2, :], 2 * shift
            pool.wait_ge(y_done, HEADS)
            for g in range(GROUPS):
                pool.memset(cbuf[:, g, :], 0.0).then_inc(ysum_own, 1)
            for j in range(DK):
                pool.wait_ge(ysq_ready, j + 1)
                pool.wait_ge(ysum_own, 2 + j)
                pool.tensor_tensor(cbuf[:, j // 4, :], cbuf[:, j // 4, :], ebuf[:, j % 2, :],
                                   ALU.add).then_inc(ysum_own, 1)
            for j in range(DK):
                pool.wait_ge(grstd_ready, j // 4 + 1)
                pool.tensor_tensor(xsT[:, cols(j)], xsT[:, cols(j)], cbuf[:, j // 4, :],
                                   ALU.mult).then_inc(yn_ready, 1)
            sum_squares(2)
            gates(1)
            sum_squares(3, DK - 1)

        @blk.scalar
        def _(act):
            def convert(m, i=0):
                act.wait_ge(landed[slot(m)], use(m, i))
                if not (isinstance(i, int) and m + RING * i < RING):
                    act.wait_ge(unit_done, i * RING + (m - RING + 1))
                act.activation(whi[:, slot(m)], raw[:, slot(m)], ACT.Copy).then_inc(w_hi, 1)

            def norm_hi(p, d, gain):
                act.wait_ge(x_ready, d + (DK * p + 1))
                act.activation(xghi[:, cols(d)], xT[:, cols(d)], ACT.Copy,
                               scale=par[:, one(d + gain)]).then_inc(xg_hi, 1)

            def square(p, d, e, x):
                if p:
                    act.wait_ge(rstd_ready, p)
                act.wait_ge(x_ready, d + (DK * p + 1))
                if not (isinstance(d, int) and p == 0 and d < 2):
                    act.wait_ge(sum_own, d + (DK + 1) * p)
                act.activation(sq[:, e, :], x, ACT.Square).then_inc(sq_ready, 1)

            def rms(p):
                act.wait_ge(stat_ready, p + 1)
                act.activation(sq[:, 0, :], PB[6][:, :], ACT.Sqrt, bias=eps[:, 0:1],
                               scale=1.0 / D).then_inc(std_ready, 1)

            def gate_up(f, m0, i, split=0):
                for j in range(4):
                    e, hidden = j // 2, i * 2 + (FT * f + j // 2)
                    if j % 2 == 0:
                        act.wait_ge(g_scaled, hidden + 1)
                        act.activation(gsilu[:, e, :], gscaled[:, e, :], ACT.Silu).then_inc(g_silu, 1)
                    else:
                        act.wait_ge(act_ready, hidden + 1)
                        act.activation(acthi[:, cols(i * 2 + e)], act32[:, e, :], ACT.Copy).then_inc(act_hi, 1)
                    if j >= split:
                        convert(m0 + j + RING, i)

            for i in range(DK // 2):
                two = slice(2 * i * P, 2 * (i + 1) * P)
                act.dma_start(xload[:, :, two],
                              t["x"][0, :, two].rearrange("(c p) f -> p c f", p=P)).then_inc(x_landed[i], 16)
            act.wait_ge(par_T, 1)
            act.activation(par[:, 0:DK], PB[7][:, 0:DK], ACT.Copy).then_inc(par_ready, 1)
            act.wait_ge(consts, 4)
            act.wait_ge(par_ready, 1)
            for i in range(DK // 2):
                for d in (2 * i, 2 * i + 1):
                    norm_hi(0, d, R_N1)
                if i % 2:
                    convert(i // 2)
                for d in ((0, 1), (), (2, 3), (4, 5))[i]:
                    square(0, d, d % 2, xT[:, cols(d)])
            convert(2)
            for d in (6, 7):
                square(0, d, d % 2, xT[:, cols(d)])
            act.wait_ge(par_T, 2)
            act.activation(par[:, DK:], PB[7][:, DK:R_ALL], ACT.Copy).then_inc(par_ready, 1)
            for m in range(3, RING + 2):
                convert(m)
            rms(0)
            gate_up(0, M_FFN1, 0, split=2)
            with act.Fori(1, FT // 2) as i:
                gate_up(0, M_FFN1, i)
            with act.Fori(0, DK // 2) as i:
                for e in range(2):
                    for j in range(4):
                        if j == 3:
                            square(1, i * 2 + e, e, xT[:, cols(i * 2 + e)])
                            norm_hi(1, i * 2 + e, R_MIX)
                        convert(N_GU + 4 * e + j + RING, i * 2)

            M = M_MIX
            rms(1)
            convert(M + U_DT + RING)

            def silu(i):
                tile = CONV_ORDER[i]
                dst = (xsT[:, cols(tile)] if tile < DK else
                       bT[:, tile - DK, :] if tile < DK + GROUPS else cT[:, tile - DK - GROUPS, :])
                act.wait_ge(conv_sum, i + 1)
                act.activation(dst, conv[:, i % 2, PAD:], ACT.Silu).then_inc(silu_done, 1)

            def exps(h):
                act.wait_ge(d_ready, h + 1)
                act.activation(cbuf[:, h % 2, CH:], PB[4 + h % 2][:, CH:], ACT.Exp).then_inc(ea_ready, 1)
                act.activation(ebuf[:, h % 2, :], ebuf[:, h % 2, :], ACT.Exp).then_inc(e_ready, 1)

            for i, tile in enumerate(CONV_ORDER):
                m = U_CONV + i
                convert(M + m + RING)
                if i >= 2:
                    act.wait_ge(silu_done, i - 1)
                act.wait_ge(proj_read, m + 1)
                act.activation(conv[:, i % 2, PAD:], proj[:, i % 2, PAD:], ACT.Identity,
                               bias=par[:, R_CB + tile:R_CB + tile + 1],
                               scale=par[:, R_CW + 3 * CT + tile:R_CW + 3 * CT + tile + 1]).then_inc(conv_id, 1)
                act.activation(ebuf[:, i % 2, :], proj[:, i % 2, PAD - 3:PAD + S - 3], ACT.Copy,
                               scale=par[:, R_CW + tile:R_CW + tile + 1]).then_inc(tap_ready, 1)
                if i:
                    silu(i - 1)
                if m == 3:
                    act.wait_ge(alog_landed, 48)
                    act.activation(a_exp[:, :], a_exp[:, :], ACT.Exp).then_inc(aexp_ready, 1)
                    act.wait_ge(abs_ready, 1)
                    act.activation(sm("e"), sm("absv"), ACT.Exp, scale=-1.0).then_inc(exp_ready, 1)
                if m == 5:
                    act.wait_ge(sel_made, 1)
                    act.activation(sel[:, :, :], sel32[:, :, :], ACT.Copy).then_inc(sel_ready, 1)
                if m == 6:
                    act.wait_ge(scr_read, SC["acs"] + 1)
                    act.activation(acs_split[:, :], acsT[:, :], ACT.Copy).then_inc(acs_hi, 1)
                if m == 8:
                    act.wait_ge(decay_in, 1)
                    act.activation(sm("wst"), sm("wst"), ACT.Exp).then_inc(decay_ready, 1)
                    act.activation(sm("tot"), sm("tot"), ACT.Exp).then_inc(decay_ready, 1)
            exps(0)
            silu(CT - 1)

            def split_hi(i):
                if i == 3:
                    pool_output(act, 1)
                elif i == 2:
                    act.wait_ge(a_bc, HEADS)
                else:
                    act.wait_ge(y_done, DK)
                for k in range(2):
                    act.wait_ge(pooled_ready, 2 * i + k + 1)
                    act.activation(splits[i][0][k][:, :], pooled[:, cols(U_ORDER[2 * i + k])],
                                   ACT.Copy).then_inc(sp_hi, 1)

            for h in range(HEADS):
                convert(M + U_Z + h + RING)
                if h + 1 < HEADS:
                    exps(h + 1)
                if h in SPLIT_AT:
                    split_hi(SPLIT_AT.index(h))
            for g in range(4):
                for d in range(2):
                    q, tile = 2 * g + d, U_ORDER[2 * g + d]
                    pool_output(act, q)
                    act.activation(xghi[:, cols(tile)], PB[POOL_BANKS[q]][:, :], ACT.Copy,
                                   scale=par[:, R_PS + tile:R_PS + tile + 1]).then_inc(pool_hi, 1)
                if g == 0:
                    split_hi(3)
                if g % 2:
                    convert(M + U_POOL + g // 2 + RING)
            for j in range(DK):
                act.activation(zT[:, cols(j)], zT[:, cols(j)], ACT.Silu).then_inc(sz_ready, 1)
            for j in range(DK):
                act.wait_ge(yg_ready, j + 1)
                if j >= 2:
                    act.wait_ge(ysum_own, 1 + j)
                act.activation(ebuf[:, j % 2, :], xsT[:, cols(j)], ACT.Square).then_inc(ysq_ready, 1)
                if j % 4 == 3:
                    convert(M + U_OUTP + j // 4 + RING)
            convert(M + U_OUTP + 2 + RING)
            convert(M + U_OUTP + 3 + RING)
            for g in range(GROUPS):
                n = SC[f"stat{g}"]
                act.wait_ge(scr_ready, n + 1)
                act.activation(cbuf[:, g, :], PB[2 + n % 2][:, :], ACT.Sqrt,
                               bias=eps[:, 0:1], scale=1.0 / (HG * HD)).then_inc(grms_ready, 1)
            for i in range(4):
                for j in (2 * i, 2 * i + 1):
                    act.wait_ge(yn_ready, j + 1)
                    act.activation(mixhi[:, cols(j)], xsT[:, cols(j)], ACT.Copy,
                                   scale=par[:, R_SSDN + j:R_SSDN + j + 1]).then_inc(mix_hi, 1)
                convert(M + U_OUTP + 4 + i + RING)
            with act.Fori(0, 2) as i:
                for j in range(4):
                    square(2, i * 4 + j, j % 2, xT[:, cols(i * 4 + j)])
                    norm_hi(2, i * 4 + j, R_N2)
                    convert(M + U_OUTS + j + RING, i)
            rms(2)
            gate_up(1, M_FFN2, 0)
            with act.Fori(1, FT // 2) as i:
                gate_up(1, M_FFN2, i)
            act.wait_ge(g_silu, 2 * FT)
            act.dma_start(gain_out, t["final_norm"].partition_broadcast(P)).then_inc(gain_landed, 16)

            def down(i, last=False):
                for e in range(1 if last else 2):
                    for j in range(4):
                        convert(M_FFN2 + N_GU + 4 * e + j + RING, i * 2)
                        if j == 3:
                            square(3, i * 2 + e, e, xnew[:, e, :])

            with act.Fori(0, DK // 2 - 1) as i:
                down(i)
            down(DK // 2 - 1, last=True)
            act.wait_ge(sum_own, (DK + 1) * 3 + DK - 1)
            for h in range(2):
                act.wait_ge(half_ready, h + 1)
                act.activation(sq[:, 1, half(h)], xnew[:, 1, half(h)], ACT.Square).then_inc(half_sq, 1)
                two = slice(2 * h, 2 * h + 2)
                act.wait_ge(tstat, h + 1)
                act.activation(tok_rms[:, 0, two], PB[LAST_STAT[h]][:, 0:2], ACT.Sqrt,
                               bias=eps[:, 0:1], scale=1.0 / D).then_inc(tstd, 1)
                act.wait_ge(trstd, h + 1)
                act.wait_ge(tok_read, DK + h)
                c = 2 * h + 1
                act.activation(xtok[:, c, :], xtok[:, c, :], ACT.Copy,
                               scale=tok_rms[:, 1, c:c + 1]).then_inc(out_odd, 1)

        @blk.vector
        def _(dve):
            chain = [0]

            def link(ins):
                chain[0] += 1
                ins.then_inc(dve_own, 1)
                dve.wait_ge(dve_own, chain[0])

            def convert(m, i=0):
                dve.wait_ge(w_hi, i * RING + (m + 1))
                dve.tensor_tensor(wlo[:, slot(m)], raw[:, slot(m)], whi[:, slot(m)].bitcast(F32),
                                  ALU.subtract).then_inc(w_lo, 1)

            def norm_lo(p, d, gain):
                dve.wait_ge(xg_hi, d + (DK * p + 1))
                dve.scalar_tensor_tensor(out=xglo[:, cols(d)], in0=xT[:, cols(d)], scalar=par[:, one(d + gain)],
                                         in1=xghi[:, cols(d)].bitcast(F32), op0=ALU.mult,
                                         op1=ALU.subtract).then_inc(xg_lo, 1)

            def inverse(p):
                dve.wait_ge(std_ready, p + 1)
                dve.reciprocal(rstd[:, :], sq[:, 0, :]).then_inc(rstd_ready, 1)
                dve.wait_ge(rstd_ready, p + 1)

            def gate_up(f, m0, i, split=0):
                for j in range(4):
                    e, hidden = j // 2, i * 2 + (FT * f + j // 2)
                    dve.wait_ge(unit_done, i * RING + (m0 + j + 1))
                    if j % 2 == 0:
                        dve.tensor_tensor(gscaled[:, e, :], PB[j][:, :], rstd[:, :], ALU.mult).then_inc(g_scaled, 1)
                    else:
                        dve.wait_ge(g_r, hidden + 1)
                        dve.tensor_tensor(act32[:, e, :], PB[j][:, :], gsilu[:, e, :],
                                          ALU.mult).then_inc(act_ready, 1)
                        dve.wait_ge(act_hi, hidden + 1)
                        dve.tensor_tensor(actlo[:, cols(i * 2 + e)], act32[:, e, :],
                                          acthi[:, cols(i * 2 + e)].bitcast(F32), ALU.subtract).then_inc(act_lo, 1)
                    if j >= split:
                        convert(m0 + j + RING, i)

            def move(*tiles):
                for d in tiles:
                    dve.wait_ge(x_in, d + 1)
                    dve.tensor_copy(xT[:, cols(d)], PB[d][:, :]).then_inc(x_ready, 1)

            for pair in ((0, 1), (2, 3)):
                move(*pair)
                for d in pair:
                    norm_lo(0, d, R_N1)
            move(4, 5)
            convert(0)
            move(6, 7)
            for d in range(4, DK):
                norm_lo(0, d, R_N1)
            for m in range(1, RING + 2):
                convert(m)
            inverse(0)
            gate_up(0, M_FFN1, 0, split=2)
            with dve.Fori(1, FT // 2) as i:
                gate_up(0, M_FFN1, i)

            with dve.Fori(0, DK // 2) as i:
                for e in range(2):
                    for j in range(4):
                        d = i * 2 + e
                        if j == 3:
                            dve.wait_ge(unit_done, i * 8 + (N_GU + 4 * e + 4))
                            dve.scalar_tensor_tensor(out=xT[:, cols(d)], in0=PB[4 + e][:, :], scalar=0.5,
                                                     in1=xT[:, cols(d)], op0=ALU.mult, op1=ALU.add).then_inc(x_ready, 1)
                            norm_lo(1, d, R_MIX)
                        convert(N_GU + 4 * e + j + RING, i * 2)

            M = M_MIX

            def scratch(n):
                dve.wait_ge(scr_ready, n + 1)
                return PB[2 + n % 2]

            def project(q, dst):
                dve.wait_ge(unit_done, M + q + 1)
                rows = dst.shape[0]
                dve.tensor_tensor(dst, PB[q % 2][0:rows, :], rstd[0:rows, :], ALU.mult).then_inc(proj_read, 1)

            def log1p_atanh():
                dve.wait_ge(exp_ready, 1)
                link(dve.tensor_scalar(sm("den"), sm("e"), 2.0, None, ALU.add))
                link(dve.reciprocal(sm("den"), sm("den")))
                link(dve.tensor_tensor(sm("t"), sm("e"), sm("den"), ALU.mult))
                link(dve.tensor_tensor(sm("t2"), sm("t"), sm("t"), ALU.mult))
                link(dve.tensor_scalar(sm("q"), sm("t2"), 1.0 / 17, None, ALU.mult))
                for odd in (15, 13, 11, 9, 7, 5, 3):
                    link(dve.scalar_tensor_tensor(out=sm("q"), in0=sm("q"), scalar=1.0 / odd, in1=sm("t2"),
                                                  op0=ALU.add, op1=ALU.mult))
                link(dve.scalar_tensor_tensor(out=sm("q"), in0=sm("q"), scalar=1.0, in1=sm("t"),
                                              op0=ALU.add, op1=ALU.mult))
                link(dve.tensor_scalar(sm("v"), sm("v"), 0.0, None, ALU.max))
                link(dve.scalar_tensor_tensor(out=sm("dt"), in0=sm("q"), scalar=2.0, in1=sm("v"),
                                              op0=ALU.mult, op1=ALU.add))
                dve.wait_ge(aexp_ready, 1)
                dve.wait_ge(pads, 3)
                for copy in range(2):
                    product = dve.scalar_tensor_tensor(
                        out=a2[:, :, copy * LOW:copy * LOW + HEADS], in0=sm3("dt"), scalar=-1.0,
                        in1=a_exp[:, :].unsqueeze(1).to_broadcast([P, NC, HEADS]), op0=ALU.mult, op1=ALU.mult)
                product.then_inc(a_ready, 1)

            def x_times_dt(j):
                w = sm3("dt")[:, :, 2 * j:2 * j + 2].unsqueeze(3).to_broadcast([P, NC, 2, HD])
                dve.tensor_tensor(xdt[:, j, :, :].rearrange("p c (e q) -> p c e q", e=2),
                                  scratch(SC[f"x{j}"])[:, :].rearrange("p (c e q) -> p c e q", c=NC, e=2),
                                  w, ALU.mult).then_inc(scr_read, 1)

            def state(g, c):
                n = SC[f"state{g}{c}"]
                bank = scratch(n)
                if c == 0:
                    dve.tensor_copy(prev[:, g, 0, :], bank[:, :]).then_inc(scr_read, 1)
                else:
                    if c == 1:
                        dve.wait_ge(decay_ready, 2)
                    dec = sm3("tot")[:, c, HG * g:HG * (g + 1)].unsqueeze(2).to_broadcast([P, HG, HD])
                    view = lambda k: prev[:, g, k, :].rearrange("p (h q) -> p h q", h=HG)
                    link(dve.tensor_tensor(view(c), view(c - 1), dec, ALU.mult))
                    dve.tensor_tensor(prev[:, g, c, :], prev[:, g, c, :], bank[:, :], ALU.add).then_inc(scr_read, 1)
                dve.wait_ge(scr_read, n + 1)

            def difference(h):
                dve.wait_ge(a_bc, h + 1)
                if h >= 2:
                    dve.wait_ge(y_done, h // 2 * 2)
                for c in range(NC):
                    exponent = dve.tensor_scalar(ebuf[:, h % 2, block(c)], PB[4 + h % 2][:, block(c)],
                                                 sm3("acs")[:, c, h:h + 1], 0.0, ALU.subtract, ALU.min)
                exponent.then_inc(d_ready, 1)

            def weigh(h):
                g = h // HG
                dve.wait_ge(e_ready, h + 1)
                dve.tensor_tensor(ebuf[:, h % 2, :], ebuf[:, h % 2, :], gm[:, g, :], ALU.mult).then_inc(m_ready, 1)
                dve.wait_ge(ea_ready, h + 1)
                dve.tensor_tensor(cbuf[:, h % 2, CH:], cbuf[:, h % 2, CH:], cT[:, g, CH:],
                                  ALU.mult).then_inc(ce_ready, 1)

            def skip(p):
                dve.wait_ge(y_done, 2 * p + 2)
                dve.scalar_tensor_tensor(out=xsT[:, cols(p)], in0=xsT[:, cols(p)],
                                         scalar=skip_col[:, p:p + 1], in1=PB[6 + p % 2][:, :],
                                         op0=ALU.mult, op1=ALU.add).then_inc(y_read, 1)

            def pool_mean(i):
                tile = U_ORDER[i]
                n = WINDOWS[tile // 2] - 1
                total = conv[:, (doublings(i) - 1) % 2, :]
                frame = proj[:, i % 2, :]
                dve.wait_ge(win_ready, i + 1)
                dve.scalar_tensor_tensor(out=pooled[:, tile * S + n:(tile + 1) * S], in0=total[:, PAD + n:],
                                         scalar=1.0 / (n + 1), in1=frame[:, PAD + n:], op0=ALU.mult, op1=ALU.subtract)
                head = pooled[:, tile * S:tile * S + n]
                link(dve.tensor_tensor(head, total[:, PAD:PAD + n], inv_count[:, 0:n], ALU.mult))
                dve.tensor_tensor(head, head, frame[:, PAD:PAD + n], ALU.subtract).then_inc(pooled_ready, 1)

            def split_lo(i):
                for k in range(2):
                    dve.wait_ge(sp_hi, 2 * i + k + 1)
                    dve.tensor_tensor(splits[i][1][k][:, :], pooled[:, cols(U_ORDER[2 * i + k])],
                                      splits[i][0][k][:, :].bitcast(F32), ALU.subtract).then_inc(sp_lo, 1)

            inverse(1)
            project(U_DT, dtfm[:, :])
            convert(M + U_DT + RING)
            dve.wait_ge(proj_read, 1)
            dve.wait_ge(alog_landed, 48)
            dve.tensor_scalar(dtfm[:, :], dtfm[:, :], dt_bias[:, 0:1], None, ALU.add).then_inc(dt_fm_ready, 1)
            pairs = skip_row[:, :].rearrange("p (j e) -> p j e", e=2)
            for e in range(2):
                rows = slice(e * HD, (e + 1) * HD)
                link(dve.tensor_copy(skip_col[rows, :], pairs[rows, :, e]))
            dve.wait_ge(pads, 2)
            dve.wait_ge(consts, 4 + PAD)
            for i, tile in enumerate(CONV_ORDER):
                m = U_CONV + i
                if m == 12:
                    state(0, 0)
                    state(0, 1)
                if i >= 2:
                    dve.wait_ge(tap_ready, i - 1)
                project(m, proj[:, i % 2, PAD:])
                if m == 12:
                    dve.wait_ge(conv_sum, i)
                    difference(0)
                convert(M + m + RING)
                dve.wait_ge(conv_id, i + 1)
                for tap in range(1, TAPS - 1):
                    back = TAPS - 1 - tap
                    r = R_CW + tap * CT + tile
                    stt = dve.scalar_tensor_tensor(
                        out=conv[:, i % 2, PAD:], in0=proj[:, i % 2, PAD - back:PAD + S - back], scalar=par[:, r:r + 1],
                        in1=conv[:, i % 2, PAD:], op0=ALU.mult, op1=ALU.add)
                    if tap < TAPS - 2:
                        link(stt)
                    else:
                        stt.then_inc(conv_done, 1)
                if m == 2:
                    dve.tensor_copy(sm("v"), scratch(SC["dt"])[:, 0:NC * HEADS]).then_inc(scr_read, 1)
                    dve.wait_ge(scr_read, SC["dt"] + 1)
                    dve.scalar_tensor_tensor(out=sm("absv"), in0=sm("v"), scalar=-1.0, in1=sm("v"),
                                             op0=ALU.mult, op1=ALU.max).then_inc(abs_ready, 1)
                if m in (3, 4):
                    dve.tensor_copy(btok[:, m - 3, :], scratch(SC[f"b{m - 3}"])[:, :]).then_inc(scr_read, 1)
                if m == 3:
                    log1p_atanh()
                if m == 5:
                    dve.tensor_copy(acsT[:, :], scratch(SC["acs"])[0:SPLIT, :]).then_inc(scr_read, 1)
                if m == 7:
                    dve.wait_ge(acs_hi, 1)
                    low = slice(LOW, SPLIT)
                    dve.tensor_tensor(acs_split[low, :], acsT[low, :], acs_split[low, :].bitcast(F32),
                                      ALU.subtract).then_inc(acs_lo, 1)
                    bank = scratch(SC["col"])
                    link(dve.tensor_copy(sm("acs"), bank[:, NC * HEADS:2 * NC * HEADS]))
                    dve.tensor_copy(sm("tot"), bank[:, 0:NC * HEADS]).then_inc(scr_read, 1)
                    dve.wait_ge(scr_read, SC["col"] + 1)
                    link(dve.tensor_tensor(sm("wst"), sm("tot"), sm("acs"), ALU.subtract))
                    dve.tensor_scalar(sm("wst"), sm("wst"), 0.0, None, ALU.min).then_inc(decay_in, 1)
                if 7 <= m <= 10:
                    x_times_dt(m - 7)
                if m == 10:
                    for g in range(GROUPS):
                        dve.wait_ge(g_mm, g + 1)
                        dve.tensor_tensor(gm[:, g, :].rearrange("p (c l) -> p c l", c=NC),
                                          PB[4 + g][:, :].rearrange("p (c l) -> p c l", c=NC),
                                          causal[:, :].unsqueeze(1).to_broadcast([P, NC, CH]), ALU.mult).then_inc(gm_ready, 1)
                if m == 12:
                    state(0, 2)
            for h in range(HEADS):
                m = U_Z + h
                if h % 2 == 0:
                    weigh(h)
                    if h:
                        skip(h // 2 - 1)
                if h < DK:
                    project(m, zT[:, cols(h)])
                else:
                    u = h - DK
                    dve.wait_ge(unit_done, M + m + 1)
                    if u >= 2:
                        dve.wait_ge(pooled_ready, u - 1)
                    dve.tensor_tensor(proj[:, u % 2, PAD:], PB[m % 2][:, :], rstd[:, :],
                                      ALU.mult).then_inc(proj_read, 1)
                if h < 4:
                    x_times_dt(4 + h)
                if h == 5:
                    state(1, 0)
                    state(1, 1)
                if h == 6:
                    state(1, 2)
                if h == 0:
                    dve.wait_ge(conv_sum, CT)
                if h % 2 == 0:
                    difference(h + 1)
                convert(M + m + RING)
                if h % 2 == 0:
                    weigh(h + 1)
                elif h + 1 < HEADS:
                    difference(h + 1)
                if h > DK:
                    pool_mean(h - DK - 1)
                if h in SPLIT_AT:
                    split_lo(SPLIT_AT.index(h))
            pool_mean(DK - 1)
            skip(DK - 1)
            split_lo(3)
            for g in range(4):
                for d in range(2):
                    q, tile = 2 * g + d, U_ORDER[2 * g + d]
                    dve.wait_ge(pool_hi, q + 1)
                    dve.scalar_tensor_tensor(out=xglo[:, cols(tile)], in0=PB[POOL_BANKS[q]][:, :],
                                             scalar=par[:, R_PS + tile:R_PS + tile + 1],
                                             in1=xghi[:, cols(tile)].bitcast(F32),
                                             op0=ALU.mult, op1=ALU.subtract).then_inc(pool_lo, 1)
                if g % 2:
                    convert(M + U_POOL + g // 2 + RING)
            for j in range(DK):
                dve.wait_ge(sz_ready, j + 1)
                dve.tensor_tensor(xsT[:, cols(j)], xsT[:, cols(j)], zT[:, cols(j)], ALU.mult).then_inc(yg_ready, 1)
            for d in range(DK):
                dve.wait_ge(unit_done, M + U_OUTP + d + 1)
                dve.tensor_tensor(xT[:, cols(d)], PB[(U_OUTP + d) % 2][:, :], xT[:, cols(d)],
                                  ALU.add).then_inc(proj_read, 1)
                if d >= 4:
                    for j in (2 * (d - 4), 2 * (d - 4) + 1):
                        dve.wait_ge(mix_hi, j + 1)
                        dve.scalar_tensor_tensor(out=mixlo[:, cols(j)], in0=xsT[:, cols(j)],
                                                 scalar=par[:, R_SSDN + j:R_SSDN + j + 1],
                                                 in1=mixhi[:, cols(j)].bitcast(F32),
                                                 op0=ALU.mult, op1=ALU.subtract).then_inc(mix_lo, 1)
                convert(M + U_OUTP + d + RING)
                if d == 3:
                    for g in range(GROUPS):
                        dve.wait_ge(grms_ready, g + 1)
                        dve.reciprocal(cbuf[:, g, :], cbuf[:, g, :]).then_inc(grstd_ready, 1)
            with dve.Fori(0, 2) as i:
                for j in range(4):
                    d = i * 4 + j
                    dve.wait_ge(unit_done, d + (M + U_OUTS + 1))
                    dve.tensor_tensor(xT[:, cols(d)], PB[4 + j % 2][:, :], xT[:, cols(d)],
                                      ALU.add).then_inc(x_ready, 1)
                    norm_lo(2, d, R_N2)
                    convert(M + U_OUTS + j + RING, i)
            inverse(2)
            gate_up(1, M_FFN2, 0)
            with dve.Fori(1, FT // 2) as i:
                gate_up(1, M_FFN2, i)

            def tokens(d, e):
                dve.wait_ge(tok_ready, d + 1)
                dve.tensor_tensor(xtok[:, :, block(d)], PB[6 + e][:, :].rearrange("p (c f) -> p c f", c=NC),
                                  gain_out[:, block(d)].unsqueeze(1).to_broadcast([P, NC, P]), ALU.mult).then_inc(tok_read, 1)

            def down(i, last=False):
                for e in range(1 if last else 2):
                    d = i * 2 + e
                    for j in range(4):
                        m = N_GU + 4 * e + j
                        if j == 1 and not (isinstance(i, int) and i == 0 and e == 0):
                            tokens(d - 1, 1 - e)
                        if j == 3:
                            dve.wait_ge(unit_done, i * 8 + (M_FFN2 + m + 1))
                            if not (isinstance(i, int) and i == 0):
                                dve.wait_ge(sq_ready, d + (3 * DK - 1))
                            dve.scalar_tensor_tensor(out=xnew[:, e, :], in0=PB[4 + e][:, :], scalar=0.5,
                                                     in1=xT[:, cols(d)], op0=ALU.mult, op1=ALU.add).then_inc(x_ready, 1)
                        convert(M_FFN2 + m + RING, i * 2)

            dve.wait_ge(gain_landed, 16)
            down(0)
            with dve.Fori(1, DK // 2 - 1) as i:
                down(i)
            down(DK // 2 - 1, last=True)
            tokens(DK - 2, 0)
            d = DK - 1
            dve.wait_ge(sq_ready, 4 * DK - 2)
            for h in range(2):
                dve.wait_ge(half_done, h + 1)
                dve.scalar_tensor_tensor(out=xnew[:, 1, half(h)], in0=PB[LAST_BANK[h]][:, 0:HALF], scalar=0.5,
                                         in1=xT[:, d * S + h * HALF:d * S + (h + 1) * HALF],
                                         op0=ALU.mult, op1=ALU.add).then_inc(half_ready, 1)
                two = slice(2 * h, 2 * h + 2)
                dve.wait_ge(half_tok, h + 1)
                dve.tensor_tensor(xtok[:, two, block(d)],
                                  PB[LAST_TOKENS[h]][:, 0:HALF].rearrange("p (c f) -> p c f", c=2),
                                  gain_out[:, block(d)].unsqueeze(1).to_broadcast([P, 2, P]), ALU.mult).then_inc(tok_read, 1)
                dve.wait_ge(tstd, h + 1)
                dve.reciprocal(tok_rms[:, 1, two], tok_rms[:, 0, two]).then_inc(trstd, 1)
                dve.wait_ge(trstd, h + 1)
                dve.wait_ge(tok_read, DK + h)
                c = 2 * h
                dve.tensor_scalar(xtok[:, c, :], xtok[:, c, :], tok_rms[:, 1, c:c + 1], None,
                                  ALU.mult).then_inc(out_even, 1)

        @blk.tensor
        def _(pe):
            def products(bank, m, i, blocks, hi, lo, k0, first=True, last=True, ready=None,
                         order=None, midway=None, width=P):
                pe.wait_ge(w_hi, i * RING + (m + 1))
                pe.wait_ge(w_lo, i * RING + (m + 1))
                s = slot(m)
                for n, k in enumerate(order or range(blocks)):
                    if midway and n == blocks // 2:
                        midway()
                    if ready:
                        pe.wait_ge(ready[0], ready[1] + n + 1)
                    h, l = hi[:, cols(k0 + k)], lo[:, cols(k0 + k)]
                    w, wl = whi[:, s, k, 0:width], wlo[:, s, k, 0:width]
                    pe.matmul(bank, w, h, start=first and n == 0, stop=False)
                    pe.matmul(bank, w, l, start=False, stop=False)
                    mm = pe.matmul(bank, wl, h, start=False, stop=last and n == blocks - 1)
                mm.then_inc(unit_done, 1)

            def stat(p):
                pe.wait_ge(sum_own, (DK + 1) * (p + 1))
                pe.matmul(PB[6][:, :], ones[:, :], sumsq[:, :], start=True, stop=True).then_inc(stat_ready, 1)

            def gate_up(f, m0, i):
                first = isinstance(i, int)
                for j in range(4):
                    if not first:
                        pe.wait_ge((g_scaled, act_ready)[j % 2], i * 2 + (FT * f + j // 2 - 1))
                    if first and m0 + j < 2:
                        continue
                    products(PB[j][:, :], m0 + j, i, UB, xghi, xglo, 0,
                             ready=(xg_lo, DK * 2 * f) if first and j == 0 else None)
                    if first and j == (2, 0)[f]:
                        stat(2 * f)

            def down(f, m0, i, behind=None, tiles=2):
                for e in range(tiles):
                    d = i * 2 + e
                    for j in range(4):
                        if j == 0:
                            if isinstance(i, int) and i == 0:
                                pe.wait_ge(x_ready, DK * (2 * f + 1))
                            else:
                                pe.wait_ge(x_ready, d + (DK * (2 * f + 1) - 1))
                        pe.wait_ge(act_lo, FT * f + DOWN0[j] + DOWN[j])
                        products(PB[4 + e][:, :], m0 + N_GU + 4 * e + j, i * 2, DOWN[j], acthi, actlo, DOWN0[j],
                                 first=j == 0, last=j == 3)
                        if j == 0 and behind and not (isinstance(i, int) and i == 0 and e == 0):
                            behind(d - 1, 1 - e)

            pe.wait_ge(consts, 4)
            pe.wait_ge(norm_landed, 16)
            pe.transpose(PB[7][:, 0:DK], prow[0:DK, :], ident[0:DK, 0:DK]).then_inc(par_T, 1)

            def x_tile(d):
                pe.wait_ge(x_landed[d // 2], 16)
                if d == DK - 1:
                    pe.wait_ge(par_ready, 1)
                for c in range(NC):
                    mm = pe.transpose(PB[d][:, block(c)], xload[:, c, block(d)], ident[:, :])
                mm.then_inc(x_in, 1)

            def gate(m, k, w, x, **flags):
                return pe.matmul(PB[m][:, :], w[:, m, k, :], x[:, cols(k)], **flags)

            def high(k):
                pe.wait_ge(xg_hi, k + 1)
                gate(0, k, whi, xghi, start=k == 0, stop=False)

            def low(k):
                pe.wait_ge(xg_lo, k + 1)
                gate(0, k, wlo, xghi, start=False, stop=False)
                return gate(0, k, whi, xglo, start=False, stop=k == DK - 1)

            for d in range(DK):
                x_tile(d)
            pe.wait_ge(w_hi, 1)
            for k in range(4):
                high(k)
            for k in range(4):
                pe.wait_ge(xg_lo, k + 1)
                gate(0, k, whi, xglo, start=False, stop=False)
            pe.wait_ge(w_lo, 1)
            for k in range(4):
                gate(0, k, wlo, xghi, start=False, stop=False)
            for k in range(4, DK):
                high(k)
                if k % 2:
                    low(k - 1)
                    mm = low(k)
            mm.then_inc(unit_done, 1)
            pe.wait_ge(par_landed, 16 * 6)
            pe.wait_ge(x_ready, DK)
            pe.transpose(PB[7][:, 0:R_ALL], prow[0:R_ALL, :], ident[0:R_ALL, 0:R_ALL]).then_inc(par_T, 1)
            pe.wait_ge(w_hi, 2)
            for k in range(DK):
                gate(1, k, whi, xghi, start=k == 0, stop=False)
            for k in range(DK):
                gate(1, k, whi, xglo, start=False, stop=False)
            pe.wait_ge(w_lo, 2)
            for k in range(DK):
                mm = gate(1, k, wlo, xghi, start=False, stop=k == DK - 1)
            mm.then_inc(unit_done, 1)
            gate_up(0, M_FFN1, 0)
            with pe.Fori(1, FT // 2) as i:
                gate_up(0, M_FFN1, i)
            down(0, M_FFN1, 0)
            with pe.Fori(1, DK // 2) as i:
                down(0, M_FFN1, i)

            M = M_MIX

            def scratch(n):
                if n >= 2:
                    pe.wait_ge(scr_read, n - 1)
                return PB[2 + n % 2]

            def project(m, ready=None, midway=None):
                if m >= 2:
                    pe.wait_ge(proj_read, m - 1)
                products(PB[m % 2][:, :], M + m, 0, UB, xghi, xglo, 0, ready=ready, midway=midway)

            def chunks_to_tokens(bank, src, width=P, off=0, rows=P):
                for c in range(NC):
                    mm = pe.transpose(bank[:, off + c * width:off + (c + 1) * width], src[:, block(c)],
                                      ident[0:rows, 0:rows])
                return mm

            def x_to_tokens(j):
                pe.wait_ge(silu_done, 4 + j + 1)
                chunks_to_tokens(scratch(SC[f"x{j}"]), xsT[:, cols(j)]).then_inc(scr_ready, 1)

            def state_products(g, c):
                pe.wait_ge(xst_ready, 4 * (g + 1))
                bank = scratch(SC[f"state{g}{c}"])[:, :].rearrange("p (j f) -> p j f", j=4)
                pe.matmul(bank, btok[:, g, block(c)],
                          xst[:, :, c, :], start=True, stop=True).then_inc(scr_ready, 1)

            def decay_rows(h):
                if h < 2:
                    pe.wait_ge(gm_ready, h + 1)
                else:
                    pe.wait_ge(ea_ready, h - 1)
                pe.matmul(PB[4 + h % 2][:, :], sel[:, h, :], acs_split[:, :], start=True, stop=True).then_inc(a_bc, 1)

            def scan(tile):
                g = tile // (DK // GROUPS)
                if tile >= 2:
                    pe.wait_ge(y_read, tile - 1)
                pe.wait_ge(m_ready, 2 * tile + 2)
                pe.wait_ge(ce_ready, 2 * tile + 2)
                for c in range(NC):
                    for e in range(2):
                        rows = slice(e * HD, (e + 1) * HD)
                        mm = pe.matmul(PB[6 + tile % 2][rows, block(c)], xdt[:, tile, c, rows], ebuf[:, e, block(c)],
                                       start=True, stop=c == 0)
                    for e in range(2 if c else 0):
                        rows = slice(e * HD, (e + 1) * HD)
                        q = (2 * tile + e) % HG * HD
                        mm = pe.matmul(PB[6 + tile % 2][rows, block(c)], prev[:, g, c - 1, q:q + HD],
                                       cbuf[:, e, block(c)], start=False, stop=True)
                mm.then_inc(y_done, 2)

            def first_states():
                state_products(0, 0)
                state_products(0, 1)

            products(PB[U_DT][0:HEADS, :], M + U_DT, 0, UB, xghi, xglo, 0, ready=(xg_lo, DK), width=HEADS)
            stat(1)
            for i in range(CT):
                m = U_CONV + i
                if m == 12:
                    pe.wait_ge(acs_lo, 1)
                    pe.wait_ge(sel_ready, 1)
                    decay_rows(0)
                project(m, midway=first_states if m == 12 else None)
                if m == 2:
                    pe.wait_ge(dt_fm_ready, 1)
                    chunks_to_tokens(scratch(SC["dt"]), dtfm, width=HEADS, rows=HEADS).then_inc(scr_ready, 1)
                if m in (3, 4):
                    pe.wait_ge(silu_done, m - 2)
                    chunks_to_tokens(scratch(SC[f"b{m - 3}"]), bT[:, m - 3, :]).then_inc(scr_ready, 1)
                if m == 5:
                    pe.wait_ge(a_ready, 1)
                    bank = scratch(SC["acs"])
                    for c in range(NC):
                        mm = pe.matmul(bank[0:SPLIT, block(c)], a2[:, c, :], causal[:, :], start=True, stop=True)
                    mm.then_inc(scr_ready, 1)
                if m == 7:
                    pe.wait_ge(scr_read, SC["acs"] + 1)
                    bank = scratch(SC["col"])
                    pe.matmul(bank[:, 0:NC * HEADS].rearrange("p (c h) -> p c h", c=NC), ones[:, :],
                              a2[:, :, 0:HEADS], start=True, stop=True)
                    chunks_to_tokens(bank, acsT[0:HEADS, :], width=HEADS, off=NC * HEADS,
                                     rows=HEADS).then_inc(scr_ready, 1)
                if 7 <= m <= 10:
                    x_to_tokens(m - 7)
                if m == 10:
                    for g in range(GROUPS):
                        for c in range(NC):
                            mm = pe.matmul(PB[4 + g][:, block(c)], bT[:, g, block(c)], cT[:, g, block(c)],
                                           start=True, stop=True)
                        mm.then_inc(g_mm, 1)
                if m == 12:
                    state_products(0, 2)
            for h in range(HEADS):
                project(U_Z + h)
                if h < 4:
                    x_to_tokens(4 + h)
                if h == 5:
                    state_products(1, 0)
                    state_products(1, 1)
                if h == 6:
                    state_products(1, 2)
                if h + 1 < HEADS:
                    decay_rows(h + 1)
                if h % 2:
                    scan(h // 2)
            for g in range(4):
                m = M + U_POOL + g // 2
                if g % 2 == 0:
                    pe.wait_ge(w_hi, m + 1)
                    pe.wait_ge(w_lo, m + 1)
                pe.wait_ge(sp_lo, 2 * g + 2)
                hi, lo = splits[g]
                for d in range(2):
                    q = 2 * g + d
                    pe.wait_ge(*((proj_read, U_POOL - 1), (proj_read, U_POOL), (scr_read, SC["state12"]),
                                 (scr_read, SC["state12"] + 1), (ea_ready, HEADS - 1), (ea_ready, HEADS),
                                 (y_read, DK - 1), (y_read, DK))[q])
                    bank = PB[POOL_BANKS[q]][:, :]
                    for k in range(2):
                        b = (1 - g % 2) * 4 + 2 * k + d
                        pe.matmul(bank, whi[:, slot(m), b, :], hi[k][:, :], start=k == 0, stop=False)
                        pe.matmul(bank, whi[:, slot(m), b, :], lo[k][:, :], start=False, stop=False)
                        mm = pe.matmul(bank, wlo[:, slot(m), b, :], hi[k][:, :], start=False, stop=k == 1)
                    mm.then_inc(unit_done if q % 4 == 3 else pool_mm, 1)
            for d in range(DK):
                if d >= 2:
                    pe.wait_ge(proj_read, U_POOL + d - 1)
                products(PB[(U_OUTP + d) % 2][:, :], M + U_OUTP + d, 0, UB, xghi, xglo, 0,
                         ready=(pool_lo, 0) if d == 0 else None, order=U_ORDER if d == 0 else None)
                if d == 3:
                    for g in range(GROUPS):
                        pe.wait_ge(ysum_own, 2 + 4 * (g + 1))
                        pe.matmul(scratch(SC[f"stat{g}"])[:, :], ones[:, :], cbuf[:, g, :],
                                  start=True, stop=True).then_inc(scr_ready, 1)
            with pe.Fori(0, 2) as i:
                for j in range(4):
                    d = i * 4 + j
                    pe.wait_ge(x_ready, d + (2 * DK - 1))
                    products(PB[4 + j % 2][:, :], M + U_OUTS + j, i, UB, mixhi, mixlo, 0,
                             ready=(mix_lo, 0) if j == 0 else None)
            gate_up(1, M_FFN2, 0)
            with pe.Fori(1, FT // 2) as i:
                gate_up(1, M_FFN2, i)

            def to_tokens(d, e):
                pe.wait_ge(x_ready, d + (3 * DK + 1))
                if not (isinstance(d, int) and d < 2):
                    pe.wait_ge(tok_read, d - 1)
                for c in range(NC):
                    mm = pe.transpose(PB[6 + e][:, block(c)], xnew[:, e, block(c)], ident[:, :])
                mm.then_inc(tok_ready, 1)

            down(1, M_FFN2, 0, to_tokens)
            with pe.Fori(1, DK // 2 - 1) as i:
                down(1, M_FFN2, i, to_tokens)
            down(1, M_FFN2, DK // 2 - 1, to_tokens, tiles=1)

            def finish(h):
                pe.wait_ge(half_ready, h + 1)
                for c in range(2):
                    mm = pe.transpose(PB[LAST_TOKENS[h]][:, block(c)], xnew[:, 1, block(2 * h + c)], ident[:, :])
                mm.then_inc(half_tok, 1)
                pe.wait_ge(sum_own, (DK + 1) * 4 - 1)
                pe.wait_ge(half_sq, h + 1)
                for c in range(2):
                    total = PB[LAST_STAT[h]][:, c:c + 1]
                    pe.matmul(total, sumsq[:, block(2 * h + c)], ones[:, 0:1], start=True, stop=False)
                    mm = pe.matmul(total, sq[:, 1, block(2 * h + c)], ones[:, 0:1], start=False, stop=True)
                mm.then_inc(tstat, 1)

            pe.wait_ge(x_ready, 4 * DK - 2)
            pe.wait_ge(tok_read, DK - 2)
            for h in range(2):
                for j in range(4):
                    m = M_FFN2 + N_GU + 4 * (DK - 1) + j
                    pe.wait_ge(w_hi, m + 1)
                    pe.wait_ge(w_lo, m + 1)
                    for k in range(DOWN[j]):
                        t0 = (DOWN0[j] + k) * S + h * HALF
                        hi, lo = acthi[:, t0:t0 + HALF], actlo[:, t0:t0 + HALF]
                        bank = PB[LAST_BANK[h]][:, 0:HALF]
                        first, last = j == 0 and k == 0, j == 3 and k == DOWN[3] - 1
                        pe.matmul(bank, whi[:, slot(m), k, :], hi, start=first, stop=False)
                        pe.matmul(bank, whi[:, slot(m), k, :], lo, start=False, stop=False)
                        mm = pe.matmul(bank, wlo[:, slot(m), k, :], hi, start=False, stop=last)
                    if j == 0:
                        if h:
                            finish(0)
                        else:
                            to_tokens(DK - 2, 0)
                mm.then_inc(half_done, 1)
            finish(1)


_INS = ["x", "ffn1_norm", "ffn1_w_gate", "ffn1_w_up", "ffn1_w_down", "mix_norm", "w_in", "conv_w", "conv_b",
        "dt_bias", "a_log", "d_skip", "ssd_norm", "pool_w", "pool_scale", "w_out", "ffn2_norm",
        "ffn2_w_gate", "ffn2_w_up", "ffn2_w_down", "final_norm"]


def kernel(**inputs):
    import concourse.bacc as bacc
    from concourse.bass_utils import run_bass_kernel_spmd

    nc = bacc.Bacc("TRN2", target_bir_lowering=False, num_devices=1, dynamic_dma_scratch_size=1024)
    arrays, aps = {}, {}
    for name in _INS:
        a = np.ascontiguousarray(inputs[name])
        arrays["in_" + name] = a
        aps[name] = nc.dram_tensor("in_" + name, a.shape, mybir.dt.from_np(a.dtype), kind="ExternalInput").ap()
    out = nc.dram_tensor("out", (1, S, D), F32, kind="ExternalOutput").ap()
    build(nc, aps, out)
    return run_bass_kernel_spmd(nc, [arrays], core_ids=[0]).results[0]["out"]
```
